# Optimizing a Trainium2 kernel written in Bass

```python
import math
import jax, jax.numpy as jnp
from jax import lax
import numpy as np

D_MODEL = 1024
BATCH = 1
SEQ = 512
DEPTH = 2

CHUNK = 64
N_MIXERS = 2
EPS = 1e-6
MLA_HEADS = 8
QK_NOPE = 128
QK_ROPE = 64
V_HEAD = 128
Q_LORA = 384
KV_LORA = 256
ROPE_THETA = 10000.0
Q_BLOCK = 128
SSM_WIDTH = D_MODEL
SSM_GROUP = 16
SSM_GROUPS = SSM_WIDTH // SSM_GROUP
SSM_STATE = 64
DT_MIN = 1e-3
DT_MAX = 1e-1
D_FF = 2816
CONV_W = 3

N_MLA_LAYERS = (DEPTH + 1) // 2
N_SSM_LAYERS = DEPTH // 2

kernel_name = "hybrid_mla_s5_convffn_stream_encoder"

def rmsnorm(x, g):
    xf = x.astype(jnp.float32)
    y = xf * lax.rsqrt(jnp.mean(xf * xf, axis=-1, keepdims=True) + EPS)
    return (y * g.astype(jnp.float32)).astype(x.dtype)

def rope_tables(positions):
    inv = 1.0 / (ROPE_THETA ** (jnp.arange(0, QK_ROPE, 2, dtype=jnp.float32) / QK_ROPE))
    ang = positions.astype(jnp.float32)[..., None] * inv
    return jnp.cos(ang), jnp.sin(ang)

def apply_rope(x, cos, sin):
    xf = x.astype(jnp.float32)
    x1, x2 = jnp.split(xf, 2, axis=-1)
    return jnp.concatenate([x1 * cos - x2 * sin, x1 * sin + x2 * cos], axis=-1).astype(x.dtype)

def mla_mixer(h, cos, sin, w_a, g_q, g_kv, w_uq, w_ukv, w_o):
    B, S, _ = h.shape
    H = MLA_HEADS
    a = h @ w_a
    c_q, c_kv, k_rope = jnp.split(a, [Q_LORA, Q_LORA + KV_LORA], axis=-1)
    q = (rmsnorm(c_q, g_q) @ w_uq).reshape(B, S, H, QK_NOPE + QK_ROPE)
    q_nope = q[..., :QK_NOPE]
    q_rope = apply_rope(q[..., QK_NOPE:], cos[:, :, None, :], sin[:, :, None, :])
    k_rope = apply_rope(k_rope, cos, sin)
    kv = (rmsnorm(c_kv, g_kv) @ w_ukv).reshape(B, S, H, QK_NOPE + V_HEAD)
    k_nope = kv[..., :QK_NOPE]
    v = kv[..., QK_NOPE:]
    scale = (QK_NOPE + QK_ROPE) ** -0.5
    nb = S // Q_BLOCK
    key_chunk = jnp.arange(S) // CHUNK

    def block(args):
        qn, qr, i = args
        s = (jnp.einsum('bqhd,bkhd->bhqk', qn, k_nope)
             + jnp.einsum('bqhr,bkr->bhqk', qr, k_rope)).astype(jnp.float32) * scale
        q_chunk = (i * Q_BLOCK + jnp.arange(Q_BLOCK)) // CHUNK
        mask = key_chunk[None, :] <= q_chunk[:, None]
        s = jnp.where(mask[None, None], s, -jnp.inf)
        p = jax.nn.softmax(s, axis=-1).astype(v.dtype)
        return jnp.einsum('bhqk,bkhd->bqhd', p, v)

    qn_b = q_nope.reshape(B, nb, Q_BLOCK, H, QK_NOPE).transpose(1, 0, 2, 3, 4)
    qr_b = q_rope.reshape(B, nb, Q_BLOCK, H, QK_ROPE).transpose(1, 0, 2, 3, 4)
    o = lax.map(block, (qn_b, qr_b, jnp.arange(nb)))
    o = o.transpose(1, 0, 2, 3, 4).reshape(B, S, H * V_HEAD)
    return o @ w_o

def s5_mixer(h, w_in, lam_re, lam_im, log_dt, b_re, b_im, c_re, c_im, d_skip, w_glu):
    B, S, _ = h.shape
    G, P, C = SSM_GROUPS, SSM_STATE, SSM_GROUP
    u = (h @ w_in).astype(jnp.float32).reshape(B, S, G, C)
    dt = jnp.exp(log_dt.astype(jnp.float32))[:, None]
    lr = lam_re.astype(jnp.float32)
    li = lam_im.astype(jnp.float32)
    mag = jnp.exp(lr * dt)
    ar = mag * jnp.cos(li * dt)
    ai = mag * jnp.sin(li * dt)
    den = lr * lr + li * li
    nr = ar - 1.0
    coef_r = (nr * lr + ai * li) / den
    coef_i = (ai * lr - nr * li) / den
    br = b_re.astype(jnp.float32)
    bi = b_im.astype(jnp.float32)
    bbar_r = coef_r[..., None] * br - coef_i[..., None] * bi
    bbar_i = coef_r[..., None] * bi + coef_i[..., None] * br
    bu_r = jnp.einsum('bsgc,gpc->bsgp', u, bbar_r)
    bu_i = jnp.einsum('bsgc,gpc->bsgp', u, bbar_i)
    a_r = jnp.broadcast_to(ar, bu_r.shape)
    a_i = jnp.broadcast_to(ai, bu_i.shape)

    def combine(e1, e2):
        a1r, a1i, b1r, b1i = e1
        a2r, a2i, b2r, b2i = e2
        return (a2r * a1r - a2i * a1i,
                a2r * a1i + a2i * a1r,
                a2r * b1r - a2i * b1i + b2r,
                a2r * b1i + a2i * b1r + b2i)

    _, _, xr, xi = lax.associative_scan(combine, (a_r, a_i, bu_r, bu_i), axis=1)
    y = (jnp.einsum('bsgp,gcp->bsgc', xr, c_re.astype(jnp.float32))
         - jnp.einsum('bsgp,gcp->bsgc', xi, c_im.astype(jnp.float32)))
    y = y.reshape(B, S, SSM_WIDTH) + d_skip.astype(jnp.float32) * u.reshape(B, S, SSM_WIDTH)
    y = jax.nn.gelu(y).astype(h.dtype)
    val, gate = jnp.split(y @ w_glu, 2, axis=-1)
    return val * jax.nn.sigmoid(gate)

def conv_ffn(h, w_up, conv_w, conv_b, w_down):
    up = h @ w_up
    up = lax.conv_general_dilated(up, conv_w[:, None, :], window_strides=(1,),
                                  padding=[(CONV_W - 1, 0)],
                                  dimension_numbers=('NWC', 'WIO', 'NWC'),
                                  feature_group_count=2 * D_FF) + conv_b
    val, gate = jnp.split(up, 2, axis=-1)
    return (jax.nn.silu(gate) * val) @ w_down

def setup_inputs(seed: int = 0) -> dict:
    key = jax.random.key(seed)
    ks = iter(jax.random.split(key, 32))
    f32 = jnp.float32

    def nrm(shape, fan_in):
        return jax.random.normal(next(ks), shape, f32) * (fan_in ** -0.5)

    def gain(shape):
        return 1.0 + 0.02 * jax.random.normal(next(ks), shape, f32)

    Lm, Ls = N_MLA_LAYERS, N_SSM_LAYERS
    G, P, C = SSM_GROUPS, SSM_STATE, SSM_GROUP
    x = jax.random.normal(next(ks), (BATCH, SEQ, D_MODEL), f32)
    offset = jax.random.randint(next(ks), (BATCH, 1), 0, 4096, dtype=jnp.int32)
    positions = (offset + jnp.arange(SEQ, dtype=jnp.int32)[None, :]).astype(jnp.int32)

    mla_w_a = nrm((Lm, D_MODEL, Q_LORA + KV_LORA + QK_ROPE), D_MODEL)
    mla_g_q = gain((Lm, Q_LORA))
    mla_g_kv = gain((Lm, KV_LORA))
    mla_w_uq = nrm((Lm, Q_LORA, MLA_HEADS * (QK_NOPE + QK_ROPE)), Q_LORA)
    mla_w_ukv = nrm((Lm, KV_LORA, MLA_HEADS * (QK_NOPE + V_HEAD)), KV_LORA)
    mla_w_o = nrm((Lm, MLA_HEADS * V_HEAD, D_MODEL), MLA_HEADS * V_HEAD)

    ssm_w_in = nrm((Ls, D_MODEL, SSM_WIDTH), D_MODEL)
    ssm_lambda_re = -0.5 + 0.02 * jax.random.normal(next(ks), (Ls, G, P), f32)
    ssm_lambda_im = math.pi * jnp.arange(P, dtype=f32)[None, None, :] + 0.02 * jax.random.normal(next(ks), (Ls, G, P), f32)
    ssm_log_dt = jax.random.uniform(next(ks), (Ls, G), f32, math.log(DT_MIN), math.log(DT_MAX))
    ssm_b_re = nrm((Ls, G, P, C), 2 * C)
    ssm_b_im = nrm((Ls, G, P, C), 2 * C)
    ssm_c_re = nrm((Ls, G, C, P), 2 * P)
    ssm_c_im = nrm((Ls, G, C, P), 2 * P)
    ssm_d = jax.random.normal(next(ks), (Ls, SSM_WIDTH), f32)
    ssm_w_glu = nrm((Ls, SSM_WIDTH, 2 * D_MODEL), SSM_WIDTH)

    ffn_w_up = nrm((DEPTH, D_MODEL, 2 * D_FF), D_MODEL)
    ffn_conv_w = nrm((DEPTH, CONV_W, 2 * D_FF), CONV_W)
    ffn_conv_b = 0.02 * jax.random.normal(next(ks), (DEPTH, 2 * D_FF), f32)
    ffn_w_down = nrm((DEPTH, D_FF, D_MODEL), D_FF)

    g_mix = gain((DEPTH, D_MODEL))
    g_ffn = gain((DEPTH, D_MODEL))
    g_final = gain((D_MODEL,))
    return {"x": x, "positions": positions,
            "mla_w_a": mla_w_a, "mla_g_q": mla_g_q, "mla_g_kv": mla_g_kv,
            "mla_w_uq": mla_w_uq, "mla_w_ukv": mla_w_ukv, "mla_w_o": mla_w_o,
            "ssm_w_in": ssm_w_in, "ssm_lambda_re": ssm_lambda_re, "ssm_lambda_im": ssm_lambda_im,
            "ssm_log_dt": ssm_log_dt, "ssm_b_re": ssm_b_re, "ssm_b_im": ssm_b_im,
            "ssm_c_re": ssm_c_re, "ssm_c_im": ssm_c_im, "ssm_d": ssm_d, "ssm_w_glu": ssm_w_glu,
            "ffn_w_up": ffn_w_up, "ffn_conv_w": ffn_conv_w, "ffn_conv_b": ffn_conv_b,
            "ffn_w_down": ffn_w_down, "g_mix": g_mix, "g_ffn": g_ffn, "g_final": g_final}

def reference(x, positions, mla_w_a, mla_g_q, mla_g_kv, mla_w_uq, mla_w_ukv, mla_w_o,
              ssm_w_in, ssm_lambda_re, ssm_lambda_im, ssm_log_dt, ssm_b_re, ssm_b_im,
              ssm_c_re, ssm_c_im, ssm_d, ssm_w_glu, ffn_w_up, ffn_conv_w, ffn_conv_b,
              ffn_w_down, g_mix, g_ffn, g_final):
    cos, sin = rope_tables(positions)
    h = x
    for i in range(DEPTH):
        hn = rmsnorm(h, g_mix[i])
        j = i // N_MIXERS
        if i % N_MIXERS == 0:
            mix = mla_mixer(hn, cos, sin, mla_w_a[j], mla_g_q[j], mla_g_kv[j],
                            mla_w_uq[j], mla_w_ukv[j], mla_w_o[j])
        else:
            mix = s5_mixer(hn, ssm_w_in[j], ssm_lambda_re[j], ssm_lambda_im[j], ssm_log_dt[j],
                           ssm_b_re[j], ssm_b_im[j], ssm_c_re[j], ssm_c_im[j], ssm_d[j], ssm_w_glu[j])
        h = h + mix
        h = h + conv_ffn(rmsnorm(h, g_ffn[i]), ffn_w_up[i], ffn_conv_w[i], ffn_conv_b[i], ffn_w_down[i])
    return rmsnorm(h, g_final)


_drawn_inputs = setup_inputs


def setup_inputs(seed=0):
    import zlib

    import numpy as np

    out = dict(_drawn_inputs(seed))
    spreads = {}
    factors = {'mla_g_q': 8.0,
     'mla_g_kv': 8.0,
     'ssm_lambda_re': 64.0,
     'ssm_lambda_im': 18.665,
     'ssm_log_dt': 18.87,
     'ssm_b_re': 34.616,
     'ssm_b_im': 34.68,
     'ssm_c_re': 34.352,
     'ssm_c_im': 34.544,
     'ffn_conv_b': 2.787,
     'g_mix': 6.66,
     'g_ffn': 2.762,
     'g_final': 8.128}
    for name, (base, spread) in spreads.items():
        noise = np.random.default_rng([zlib.crc32(name.encode()), seed]).standard_normal(out[name].shape)
        drawn = base * np.exp(spread * noise) if base else spread * noise
        out[name] = __import__('jax').numpy.asarray(drawn.astype(out[name].dtype))
    for name, factor in factors.items():
        out[name] = (out[name] * factor).astype(out[name].dtype)
    return out
```

```python
from contextlib import ExitStack

import numpy as np
import concourse.bass as bass
from concourse import mybir

P = 128
D, S, DEPTH = 1024, 512, 2
KD = D // P
TT = S // P
EPS = 1e-6
CHUNK = 64
HEADS, NOPE, ROPE, VH = 8, 128, 64, 128
Q_LORA, KV_LORA = 384, 256
KQ, KKV = Q_LORA // P, KV_LORA // P
SCALE = float(NOPE + ROPE) ** -0.5
THETA = 10000.0
D_FF = 2816
NF = D_FF // P
THIRDS = [(0, 8), (8, 8), (16, 6)]
G, PS, C = 64, 64, 16
NQ = G // 2
LQ = S // 64
NK = S // LQ
TWO_PI = 2.0 * np.pi
MAGIC = 12582912.0
PI_1 = 6.28125
PI_2 = float(np.float32(1.9350051879882812e-03))
PI_3 = float(TWO_PI - PI_1 - PI_2)
PI_IN = 3.1415925
NEG = -3.0e38

ALU = mybir.AluOpType
ACT = mybir.ActivationFunctionType
AX = mybir.AxisListType
F32 = mybir.dt.float32
FR = mybir.dt.float32r
I32 = mybir.dt.int32

PHASES = [("wa", 6, 8), ("uq", 6, 6), ("uk", 2, 8), ("uv", 2, 8), ("wo", 8, 8)]
for _l in range(DEPTH):
    if _l == 1:
        PHASES += [("win", 8, 8), ("glu", 16, 8)]
    for _t, (_f0, _n) in enumerate(THIRDS):
        PHASES += [(f"up{_l}{_t}", 2 * _n, 8), (f"dn{_l}{_t}", KD, _n)]
ORDER = [n for n, _, _ in PHASES]
BLOCKS = {n: b for n, b, _ in PHASES}
UNITS = {n: u for n, _, u in PHASES}
FIRST = {}
_b = 0
for _n, _c, _u in PHASES:
    FIRST[_n] = _b
    _b += _c
NBLOCKS = _b

TILE0, SQ0 = {}, {}
_b = 0
for _n, _c in [("x", 8), ("c", 5), ("o", 8), ("n_wo", 8), ("h00", 8), ("h01", 8), ("h02", 6), ("n_dn02", 8),
               ("y", 8), ("n_glu", 8), ("h10", 8), ("h11", 8), ("h12", 6)]:
    TILE0[_n] = _b
    _b += _c
_b = 0
for _n, _c in [("x", 8), ("c", 5), ("n_wo", 8), ("n_dn02", 8), ("n_glu", 8), ("n_dn12", 8)]:
    SQ0[_n] = _b
    _b += _c
NORMS = ["x", "q", "kv", "n_wo", "n_dn02", "n_glu", "n_dn12"]
SQ_END = {"x": 8, "q": 8 + KQ, "kv": 13, "n_wo": 21, "n_dn02": 29, "n_glu": 37, "n_dn12": 45}
WIDTH = {"q": Q_LORA, "kv": KV_LORA}


def following(name):
    n = ORDER.index(name) + 1
    return ORDER[n] if n < len(ORDER) else None


def pair_loop(eng, pairs, body):
    body(0, pairs == 1)
    if pairs > 2:
        with eng.Fori(1, pairs - 1) as i:
            body(i, False)
    if pairs > 1:
        body(pairs - 1, True)


def build(nc, d):
    ctx = ExitStack()
    with ctx:
        base = [(nc.sbuf_base + 63) // 64 * 64]

        def place(name, shape, dt, at):
            size = 4 * int(np.prod(shape[1:]))
            assert at + size <= nc.sbuf_usable_end, (name, at + size - nc.sbuf_usable_end)
            t = nc.alloc_sbuf_tensor_at(name, list(shape), dt, offset=at)
            return t, (at + size + 31) // 32 * 32

        def keep(name, shape, dt=F32):
            t, base[0] = place(name, shape, dt, base[0])
            return t

        def sem(name):
            return ctx.enter_context(nc.semaphore(name))

        X = keep("X", [P, KD, S])
        GH = keep("GH", [P, KD, S], FR)
        GL = keep("GL", [P, KD, S], FR)
        AH = keep("AH", [P, KD, S], FR)
        AL = keep("AL", [P, KD, S], FR)
        RAW = [keep(f"RAW{i}", [P, 8 * P]) for i in range(2)]
        WH = [keep(f"WH{i}", [P, 8 * P], FR) for i in range(2)]
        WL = [keep(f"WL{i}", [P, 8 * P], FR) for i in range(2)]
        RSTD = keep("RSTD", [P, S])
        SS = keep("SS", [P, S])
        SQ = [keep(f"SQ{i}", [P, S]) for i in range(2)]
        DIAG = keep("DIAG", [P, TT, P])
        IDENT = keep("IDENT", [P, P])
        PERM = keep("PERM", [P, P])
        ONES = keep("ONES", [P, P])
        GAIN = keep("GAIN", [P, 5 * KD + KQ + KKV])
        CONV = keep("CONV", [P, DEPTH * 2 * NF, 4])
        STD = keep("STD", [P, TT])
        RCOL = keep("RCOL", [P, TT])
        RCKV = keep("RCKV", [P, TT])
        EPST = keep("EPST", [P, 1])
        INV = keep("INV", [P, 1])
        MX = keep("MX", [P, 32])
        SM = keep("SM", [P, 32])
        RS = keep("RS", [P, 32])
        DCOL = keep("DCOL", [P, G])
        small = {n: keep("s_" + n, [P, NQ]) for n in
                 ("lr", "li", "ld", "dt", "ldt", "th", "mag", "sn", "cs", "k", "r", "rden", "ar", "ai", "cr", "ci",
                  "wr", "wi", "r8", "t1", "t2", "t3")}
        A0 = base[0]

        Qn, at = place("Qn", [P, HEADS, S], F32, A0)
        Kn, at = place("Kn", [P, HEADS, S], F32, at)
        QR, at = place("QR", [P, HEADS // 2, S], F32, at)
        KR = [None, None]
        KR[0], at = place("KR0", [P, S], F32, at)
        KR[1], at = place("KR1", [P, S], F32, at)
        V, at = place("V", [P, TT, HEADS * VH], F32, at)
        attn_b = at
        COS, at = place("COS", [P, S], F32, attn_b)
        SIN, at = place("SIN", [P, S], F32, at)
        CR = [None, None]
        CR[0], at = place("CR0", [P, S], F32, at)
        CR[1], at = place("CR1", [P, S], F32, at)
        RAWR = [None, None]
        RAWR[0], at = place("RAWR0", [P, S], F32, at)
        RAWR[1], at = place("RAWR1", [P, S], F32, at)
        TMP, at = place("TMP", [P, S], F32, at)
        RSTDQ, at = place("RSTDQ", [P, S], F32, at)
        RSTDKV, at = place("RSTDKV", [P, S], F32, at)
        SSKV, at = place("SSKV", [P, S], F32, at)
        POSI, _ = place("POSI", [P, S], I32, A0)
        POSF, _ = place("POSF", [P, S], F32, A0 + 2048)
        KANG, _ = place("KANG", [P, S], F32, A0 + 4096)
        PR_, at = place("Pexp", [P, TT, S], F32, attn_b)
        PT0, at = place("PT0", [P, TT, S], F32, at)
        PT1, at = place("PT1", [P, TT, S], F32, at)
        PT = [PT0, PT1]

        PWR, at = place("PWR", [P, LQ + 1, NQ], F32, A0)
        PWI, at = place("PWI", [P, LQ + 1, NQ], F32, at)
        WC, at = place("WC", [P, NQ, NK], F32, at)
        WS, at = place("WS", [P, NQ, NK], F32, at)
        RT, at = place("RT", [P, NQ, NK], F32, at)
        CRE, at = place("CRE", [P, NQ, C], F32, at)
        CIN, at = place("CIN", [P, NQ, C], F32, at)
        BBR, at = place("BBR", [P, NQ, C], F32, at)
        BBI, at = place("BBI", [P, NQ, C], F32, at)
        CBR, at = place("CBR", [P, NQ, 2 * C], F32, at)
        CBI, at = place("CBI", [P, NQ, 2 * C], F32, at)
        GR, at = place("GR", [P, 4, LQ, C], F32, at)
        GI, at = place("GI", [P, 4, LQ, C], F32, at)
        PT1_, at = place("PT1_", [P, 4 * LQ * C], F32, at)
        PT2_, at = place("PT2_", [P, 4 * LQ * C], F32, at)
        OR, OI, ET, TM, KALL = ([None, None] for _ in range(5))
        ring0 = at
        for i in range(2):
            OR[i], at = place(f"OR{i}", [P, 4, LQ, C], F32, at)
            OI[i], at = place(f"OI{i}", [P, 4, LQ, C], F32, at)
            ET[i], at = place(f"ET{i}", [P, 2, 4, P], F32, at)
            KALL[i], at = place(f"KALL{i}", [P, 8, C], F32, at)
        BRE, _ = place("BRE", [P, NQ, C], F32, ring0)
        BIM, _ = place("BIM", [P, NQ, C], F32, ring0 + 2048)
        MASK, at = place("MASK", [P, C], F32, at)
        f0 = at
        Z, CV = [None, None], [None, None]
        for i in range(2):
            Z[i], at = place(f"Z{i}", [P, S + 2], F32, at)
            CV[i], at = place(f"CV{i}", [P, S], F32, at)
        SG, at = place("SG", [P, S], F32, at)
        HH, at = place("HH", [P, S], F32, at)
        UB, U2, Y2, YB, XR, XI = ([None, None] for _ in range(6))
        at = f0
        for i in range(2):
            U2[i], at = place(f"U2{i}", [P, 8, NK], F32, at)
            XR[i], at = place(f"XR{i}", [P, 4, NK + 1], F32, at)
            XI[i], at = place(f"XI{i}", [P, 4, NK + 1], F32, at)
        for i in range(2):
            TM[i], at = place(f"TM{i}", [P, 8, LQ, C], F32, at)
        TMR, at = place("TMR", [P, LQ, 8, C], F32, at)
        UB, at = place("UB", [P, LQ, NK], F32, at)
        Y2, at = place("Y2", [P, 8, NK], F32, at)
        YB, at = place("YB", [P, LQ, NK], F32, at)
        R4 = []
        for i in range(6):
            t, at = place(f"R4{i}", [P, 4 * NK], F32, at)
            R4.append(t)
        VAL, _ = place("VAL", [P, S], F32, f0)
        SIG, _ = place("SIG", [P, S], F32, f0 + 2048)
        ZERO, _ = place("ZERO", [112, P], F32, f0)

        bank = [ctx.enter_context(nc.psum_tensor(f"bank{i}", [P, S], F32)) for i in range(8)]

        UD = nc.dram_tensor("ud_scratch", (8, P, LQ, NK), F32, kind="Internal").ap()
        YD = nc.dram_tensor("yd_scratch", (8, P, 8, NK), F32, kind="Internal").ap()
        KDR = nc.dram_tensor("kd_scratch", (8, 15 * C, P), F32, kind="Internal").ap()

        s_raw = [sem("raw0_loaded"), sem("raw1_loaded")]
        s_hi, s_lo, s_mm, s_ev = sem("w_hi"), sem("w_lo"), sem("block_done"), sem("bank_read")
        s_thi, s_act = sem("tile_hi"), sem("tile_lo")
        s_sq, s_ss = sem("squared"), sem("sq_summed")
        s_st, s_std, s_dg, s_bc, s_rstd = sem("stat"), sem("std"), sem("diag"), sem("bcast"), sem("rstd")
        s_x = [sem(f"x{k}_loaded") for k in range(KD)]
        s_par, s_tab, s_pos, s_const = sem("gain_loaded"), sem("tables_loaded"), sem("pos_loaded"), sem("const_made")
        s_ang, s_trig = sem("angles"), sem("trig")
        s_den = sem("ssm_den")
        s_pm = sem("permuted")
        s_sc, s_mx, s_p, s_pn, s_pt, s_ptc, s_pv, s_oc = (sem(n) for n in (
            "scores", "row_max", "exps", "probs", "probs_t", "probs_t_copied", "pv", "o_read"))
        s_z, s_c, s_cv, s_sg, s_h = (sem(n) for n in ("z", "tap2", "conv", "gate", "hidden"))
        s_spar, s_zz, s_kz = sem("s5_loaded"), sem("zero_made"), sem("kd_zeroed")
        s_G, s_O, s_et, s_etc, s_kall = sem("G"), sem("O"), sem("ET"), sem("ET_copied"), sem("kall")
        s_kw, s_T, s_tm = sem("kd_written"), sem("TMR_loaded"), sem("lags_sorted")
        s_u, s_uw, s_ur = sem("u"), sem("ud_written"), [sem("U0_loaded"), sem("U1_loaded")]
        s_E, s_X, s_Y, s_g = sem("E"), sem("states"), sem("Y"), sem("gelu")
        s_yw, s_yr = sem("yd_written"), sem("YB_loaded")
        s_val, s_sig = sem("val"), sem("sigmoid")
        s_fin, s_out = sem("final"), sem("out_written")

        block = ctx.enter_context(nc.Block())

        def gain(kind, k):
            g0 = {"mix0": 0, "mix1": KD, "ffn0": 2 * KD, "ffn1": 3 * KD, "final": 4 * KD,
                  "q": 5 * KD, "kv": 5 * KD + KQ}[kind]
            if isinstance(k, int):
                return GAIN[:, g0 + k:g0 + k + 1]
            return GAIN[:, bass.ds(g0 + k, 1)]

        def one(t, k):
            if isinstance(k, int):
                return t[:, k, :]
            return t[:, bass.ds(k, 1), :].rearrange("p a s -> p (a s)")

        @block.sync
        def _(sp):
            def load(name, i, p):
                b = FIRST[name] + 2 * i + p
                n = UNITS[name] * P
                if not (isinstance(b, int) and b < 2):
                    sp.wait_ge(s_lo, b - 1)
                src = d["w_" + name]
                sp.dma_start(RAW[p][:, :n], src[2 * i + p] if isinstance(i, int) else
                             src[bass.ds(2 * i + p, 1)].rearrange("a p n -> (a p) n")).then_inc(s_raw[p], 16)

            def load_next(name, i, p, last):
                if not last:
                    load(name, i + 1, p)
                elif following(name):
                    load(following(name), 0, p)

            sp.dma_start(POSI[:], d["pos"].partition_broadcast(P)).then_inc(s_pos, 16)
            sp.dma_start(INV[:], d["inv"]).then_inc(s_pos, 16)
            for n in ("lr", "li", "ld"):
                sp.dma_start(small[n][:], d[n]).then_inc(s_pos, 16)
            load("wa", 0, 0)
            for k in range(KD):
                sp.dma_start(X[:, k, :], d["x"][k]).then_inc(s_x[k], 16)
                if k == 1:
                    sp.dma_start(GAIN[:], d["gain"]).then_inc(s_par, 16)
                    sp.dma_start(IDENT[:], d["ident"]).then_inc(s_par, 16)
                if k == 3:
                    load("wa", 0, 1)
            sp.dma_start(PERM[:], d["perm"]).then_inc(s_tab, 16)
            sp.dma_start(CONV[:], d["conv"]).then_inc(s_tab, 16)
            sp.dma_start(DCOL[:], d["dcol"]).then_inc(s_tab, 16)

            def s5_params():
                sp.wait_ge(s_mm, FIRST["wo"] + BLOCKS["wo"])
                for t, n in ((BRE, "bre"), (BIM, "bim"), (CRE, "cre"), (CIN, "cim"), (CBR, "cbr"), (CBI, "cbi"),
                             (MASK, "mask")):
                    sp.dma_start(t[:], d[n]).then_inc(s_spar, 16)

            def s5_step(i, j, p, win=True, y=True):
                if win:
                    sp.wait_ge(s_ev, FIRST["win"] + j + 1)
                    sp.dma_start(dr(UD, j), UB[:]).then_inc(s_uw, 16)
                    sp.wait_ge(s_kall, j + 1)
                    sp.dma_start(dr(KDR, j)[7 * C:15 * C, :], KALL[p][:]).then_inc(s_kw, 16)
                    if y:
                        sp.wait_ge(s_Y, j - 1)
                    sp.wait_ge(s_uw, 16 * (j + 1))
                    for s in range(LQ):
                        sp.dma_start(U2[p][C * s:C * s + C], dr(UD, j).rearrange("(g c) s k -> s c g k", g=8)[
                            LQ - 1 - s]).then_inc(s_ur[p], 16)
                    sp.wait_ge(s_kw, 16 * (j + 1))
                    k = dr(KDR, j)
                    if not (isinstance(j, int) and j == 0):
                        sp.wait_ge(s_tm, j)
                    sp.dma_start(TMR[:].rearrange("p s g c -> p s (g c)"),
                                 bass.AP(k.tensor, k.offset, [[P, P], [C * P, LQ], [1, P]])).then_inc(s_T, 16)
                if y:
                    sp.wait_ge(s_g, j - 1)
                    sp.dma_start(dr(YD, j - 2), Y2[:]).then_inc(s_yw, 16)
                    sp.wait_ge(s_yw, 16 * (j - 1))
                    if not (isinstance(j, int) and j == 2):
                        sp.wait_ge(s_act, TILE0["y"] + j - 2)
                    for g in range(8):
                        sp.dma_start(YB[C * g:C * g + C], dr(YD, j - 2).rearrange("(s c) g k -> g c s k", s=LQ)[g]
                                     ).then_inc(s_yr, 16)

            def dr(t, j):
                if isinstance(j, int):
                    return t[j]
                v = t[bass.ds(j, 1)]
                return v.rearrange("a b c -> (a b) c") if len(t.shape) == 3 else v.rearrange("a b c d -> (a b) c d")

            for name in ORDER:
                if name == "win":
                    sp.wait_ge(s_zz, 1)
                    for j in range(8):
                        sp.dma_start(KDR[j][0:7 * C, :], ZERO[:]).then_inc(s_kz, 16)
                    sp.wait_ge(s_kz, 128)

                    def steps(i, last, first=False):
                        for p in range(2):
                            load_next(name, i, p, last)
                            s5_step(i, 2 * i + p, p, y=not first)
                    steps(0, False, True)
                    steps(1, False)
                    steps(2, False)
                    steps(3, True)
                    for j in (8, 9):
                        s5_step(4, j, j % 2, win=False)
                    continue
                if name == "up00":
                    s5_params()
                pair_loop(sp, BLOCKS[name] // 2, lambda i, last: [load_next(name, i, p, last) for p in range(2)])
            for k in range(KD):
                sp.wait_ge(s_fin, k + 1)
                sp.dma_start(d["out"][k], X[:, k, :]).then_inc(s_out, 16)
            sp.wait_ge(s_out, 16 * KD)

        @block.scalar
        def _(act):
            act_ = nc.scalar.activation

            def hi(name, i, p):
                b = FIRST[name] + 2 * i + p
                n = UNITS[name] * P
                act.wait_ge(s_raw[p], 16 * (FIRST[name] // 2 + i + 1))
                if not (isinstance(b, int) and b < 2):
                    act.wait_ge(s_mm, b - 1)
                act_(WH[p][:, :n], RAW[p][:, :n], ACT.Copy).then_inc(s_hi, 1)

            def hi_next(name, i, p, last):
                if not last:
                    hi(name, i + 1, p)
                elif following(name):
                    hi(following(name), 0, p)

            def square(src, dst, key, j, p):
                if key in ("x", "c") and j >= 2:
                    act.wait_ge(s_ss, SQ0[key] + j - 1)
                act_(dst[:], src, ACT.Square).then_inc(s_sq, 1)

            def std(norm):
                act.wait_ge(s_st, NORMS.index(norm) + 1)
                act_(STD[:], bank[2][:, 0:TT], ACT.Sqrt, bias=EPST[:, 0:1],
                     scale=1.0 / WIDTH.get(norm, D)).then_inc(s_std, 1)

            sm = small
            act.wait_ge(s_pos, 16 * 5)
            act_(sm["dt"][:], sm["ld"][:], ACT.Exp).then_inc(s_trig, 1)
            hi("wa", 0, 0)
            act.wait_ge(s_par, 16 * 2)
            for k in range(KD):
                act.wait_ge(s_x[k], 16)
                act_(GH[:, k, :], X[:, k, :], ACT.Identity, scale=gain("mix0", k)).then_inc(s_thi, 1)
                square(X[:, k, :], SQ[k % 2], "x", k, k % 2)
                if k == 3:
                    hi("wa", 0, 1)
            act.wait_ge(s_const, 1)
            std("x")
            act.wait_ge(s_ang, 1)
            act_(sm["mag"][:], sm["ldt"][:], ACT.Exp).then_inc(s_trig, 1)
            for n, (dst, src) in enumerate(((COS, COS), (SIN, SIN), (sm["cs"], sm["cs"]), (sm["sn"], sm["sn"]))):
                act.wait_ge(s_ang, n + 2)
                act_(dst[:], src[:], ACT.Sin).then_inc(s_trig, 1)

            for b in range(6):
                act.wait_ge(s_mm, b + 1)
                hi_next("wa", b // 2, b % 2, b // 2 == 2)
                if b < 5:
                    act.wait_ge(s_ev, b + 1)
                    g = gain("q", b) if b < KQ else gain("kv", b - KQ)
                    act_(AH[:, b, :], CR[b % 2][:], ACT.Identity, scale=g).then_inc(s_thi, 1)
                    square(CR[b % 2][:], SQ[b % 2], "c", b, b % 2)
                if b == 4:
                    std("q")
                if b == 5:
                    std("kv")
            act.wait_ge(s_tab, 16 * 3)
            for name in ("uq", "uk", "uv"):
                for b in range(BLOCKS[name]):
                    act.wait_ge(s_mm, FIRST[name] + b + 1)
                    hi_next(name, b // 2, b % 2, b // 2 == BLOCKS[name] // 2 - 1)

            def exps(n):
                qb = n % 4
                N = (qb + 1) * P
                act.wait_ge(s_mx, n + 1)
                if n >= 4:
                    act.wait_ge(s_pt, n - 3)
                act_(PR_[:, qb, :N], bank[2 + qb][:, :N], ACT.Exp, bias=MX[:, n:n + 1],
                     accum_out=SM[:, n:n + 1]).then_inc(s_p, 1)

            def pt_copy(n):
                h, qb = n // 4, n % 4
                act.wait_ge(s_pt, n + 1)
                if h >= 2:
                    act.wait_ge(s_pv, h - 1)
                act_(PT[h % 2][:, 0:qb + 1, qb * P:(qb + 1) * P],
                     bank[6 + qb % 2][:, 0:(qb + 1) * P].rearrange("p (a b) -> p a b", a=qb + 1),
                     ACT.Copy).then_inc(s_ptc, 1)

            def o_hi(h):
                act.wait_ge(s_pv, h + 1)
                act_(AH[:, h, :], bank[h % 2][:], ACT.Copy).then_inc(s_thi, 1)

            for n in range(4 * HEADS + 5):
                if n < 4 * HEADS:
                    exps(n)
                if n >= 3 and n - 3 < 4 * HEADS:
                    pt_copy(n - 3)
                if n >= 7 and n % 4 == 0:
                    o_hi((n - 8) // 4)
            def next_tile(name, key, kind, j, p, b):
                act.wait_ge(s_ev, b + 1)
                if kind != "final":
                    act_(one(GH, j), one(X, j), ACT.Identity, scale=gain(kind, j)).then_inc(s_thi, 1)
                square(one(X, j), SQ[p], key, j, p)

            def wo(i, last):
                for p in range(2):
                    b = FIRST["wo"] + 2 * i + p
                    act.wait_ge(s_mm, b + 1)
                    hi_next("wo", i, p, last)
                    next_tile("wo", "n_wo", "ffn0", 2 * i + p, p, b)
            pair_loop(act, 4, wo)

            def ffn(l, done):
                std(done[0])
                for t, (f0, n) in enumerate(THIRDS):
                    name = f"up{l}{t}"

                    def up(i, last):
                        for p in range(2):
                            b = FIRST[name] + 2 * i + p
                            c0 = 2 * NF * l + 2 * f0
                            act.wait_ge(s_mm, b + 1)
                            hi_next(name, i, p, last)
                            act.wait_ge(s_ev, b + 1)
                            w2 = CONV[:, c0 + 2 * i + p, 2:3] if isinstance(i, int) else \
                                CONV[:, bass.ds(c0 + 2 * i + p, 1), 2:3].rearrange("p a b -> p (a b)")
                            wb = CONV[:, c0 + 2 * i + p, 3:4] if isinstance(i, int) else \
                                CONV[:, bass.ds(c0 + 2 * i + p, 1), 3:4].rearrange("p a b -> p (a b)")
                            act_(CV[p][:], Z[p][:, 2:S + 2], ACT.Identity, scale=w2, bias=wb).then_inc(s_c, 1)
                            if p == 0 and not (isinstance(i, int) and i == 0):
                                hid(i - 1)
                        act.wait_ge(s_cv, NF * l + f0 + i + 1)
                        act_(SG[:], CV[1][:], ACT.Silu).then_inc(s_sg, 1)

                    def hid(i):
                        act.wait_ge(s_h, NF * l + f0 + i + 1)
                        act_(one(AH, i), HH[:], ACT.Copy).then_inc(s_thi, 1)
                    pair_loop(act, n, up)
                    hid(n - 1)
                    dn = f"dn{l}{t}"

                    def down(i, last):
                        for p in range(2):
                            b = FIRST[dn] + 2 * i + p
                            act.wait_ge(s_mm, b + 1)
                            hi_next(dn, i, p, last)
                            if t == 2:
                                next_tile(dn, done[1], done[2], 2 * i + p, p, b)
                    pair_loop(act, KD // 2, down)

            ffn(0, ("n_wo", "n_dn02", "mix1"))

            std("n_dn02")

            def y_tile(j):
                act.wait_ge(s_yr, 128 * (j + 1))
                act_(one(AH, j).rearrange("p (k s) -> p s k", s=LQ), YB[:], ACT.Copy).then_inc(s_thi, 1)

            def gelu(j):
                act.wait_ge(s_Y, j + 1)
                if not (isinstance(j, int) and j == 0):
                    act.wait_ge(s_yw, 16 * j)
                for gi in range(2):
                    m = act_(Y2[:, gi::2, :], bank[6 + gi][:, 0:4 * NK].rearrange("p (a k) -> p a k", k=NK),
                             ACT.Gelu_apprx_tanh)
                m.then_inc(s_g, 1)

            def sort_lags(j, p):
                act.wait_ge(s_T, 16 * (j + 1))
                act_(TM[p][:].rearrange("p g s c -> p s g c"), TMR[:], ACT.Copy).then_inc(s_tm, 1)

            def s5(i, last, first=False, tail=False):
                for p in range(2):
                    j = 2 * i + p
                    if not tail:
                        act.wait_ge(s_mm, FIRST["win"] + j + 1)
                        hi_next("win", i, p, last)
                    if not first:
                        gelu(j - 2)
                    if not tail:
                        sort_lags(j, p)
                    if not first:
                        y_tile(j - 2)
            s5(0, False, first=True)
            with act.Fori(1, 3) as i:
                s5(i, False)
            s5(3, True)
            s5(4, False, tail=True)

            def glu(i, last):
                for p in range(2):
                    b = FIRST["glu"] + 2 * i + p
                    act.wait_ge(s_mm, b + 1)
                    hi_next("glu", i, p, last)
                if not (isinstance(i, int) and i == 0):
                    act.wait_ge(s_ev, b - 1)
                act_(SIG[:], bank[1][:], ACT.Sigmoid).then_inc(s_sig, 1)
                next_tile("glu", "n_glu", "ffn1", i, 0, b)
            pair_loop(act, KD, glu)

            ffn(1, ("n_glu", "n_dn12", "final"))
            std("n_dn12")

        @block.vector
        def _(dve):
            v = nc.vector

            def lo(name, i, p):
                b = FIRST[name] + 2 * i + p
                n = UNITS[name] * P
                dve.wait_ge(s_hi, b + 1)
                v.tensor_tensor(WL[p][:, :n], RAW[p][:, :n], WH[p][:, :n].bitcast(F32), ALU.subtract).then_inc(s_lo, 1)

            def lo_next(name, i, p, last):
                if not last:
                    lo(name, i + 1, p)
                elif following(name):
                    lo(following(name), 0, p)

            def add_square(key, j, p, ss=None, first=False):
                ss = ss or SS
                n = SQ0[key] + j
                dve.wait_ge(s_sq, n + 1)
                if first:
                    v.tensor_copy(ss[:], SQ[p][:]).then_inc(s_ss, 1)
                else:
                    dve.wait_ge(s_ss, n)
                    v.tensor_tensor(ss[:], ss[:], SQ[p][:], ALU.add).then_inc(s_ss, 1)

            def rstd(norm, dst, col):
                n = NORMS.index(norm)
                dve.wait_ge(s_std, n + 1)
                v.reciprocal(col[:], STD[:])
                v.drain()
                for t in range(TT):
                    m = v.tensor_scalar(DIAG[:, t, :], IDENT[:], col[:, t:t + 1], None, ALU.mult)
                m.then_inc(s_dg, 1)
                dve.wait_ge(s_bc, n + 1)
                v.tensor_copy(dst[:], bank[3][:]).then_inc(s_rstd, 1)
                v.drain()

            def reduce_angle(dst, ang, k, cosine):
                v.tensor_scalar(k[:], ang[:], 1.0 / TWO_PI, 0.25 if cosine else 0.0, ALU.mult, ALU.add)
                v.drain()
                v.tensor_scalar(k[:], k[:], MAGIC, MAGIC, ALU.add, ALU.subtract)
                v.drain()
                v.scalar_tensor_tensor(out=dst[:], in0=k[:], scalar=-PI_1, in1=ang[:], op0=ALU.mult, op1=ALU.add)
                v.drain()
                v.scalar_tensor_tensor(out=dst[:], in0=k[:], scalar=-PI_2, in1=dst[:], op0=ALU.mult, op1=ALU.add)
                v.drain()
                v.scalar_tensor_tensor(out=dst[:], in0=k[:], scalar=-PI_3, in1=dst[:], op0=ALU.mult, op1=ALU.add)
                v.drain()
                if cosine:
                    v.tensor_scalar(dst[:], dst[:], np.pi / 2, None, ALU.add)
                    v.drain()
                v.tensor_scalar(dst[:], dst[:], PI_IN, -PI_IN, ALU.min, ALU.max).then_inc(s_ang, 1)

            v.memset(ONES[:], 1.0)
            v.memset(EPST[:], EPS).then_inc(s_const, 1)
            sm = small
            dve.wait_ge(s_pos, 16 * 5)
            dve.wait_ge(s_trig, 1)
            v.tensor_tensor(sm["ldt"][:], sm["lr"][:], sm["dt"][:], ALU.mult).then_inc(s_ang, 1)
            v.tensor_tensor(sm["th"][:], sm["li"][:], sm["dt"][:], ALU.mult)
            v.tensor_copy(POSF[:], POSI[:])
            v.drain()
            v.tensor_scalar(POSF[:], POSF[:], INV[:, 0:1], None, ALU.mult)
            v.drain()
            reduce_angle(COS, POSF, KANG, True)
            reduce_angle(SIN, POSF, KANG, False)
            reduce_angle(sm["cs"], sm["th"], sm["k"], True)
            reduce_angle(sm["sn"], sm["th"], sm["k"], False)
            v.tensor_tensor(sm["t1"][:], sm["lr"][:], sm["lr"][:], ALU.mult)
            v.tensor_tensor(sm["t2"][:], sm["li"][:], sm["li"][:], ALU.mult)
            v.drain()
            v.tensor_tensor(sm["t3"][:], sm["t1"][:], sm["t2"][:], ALU.add)
            v.drain()
            v.reciprocal(sm["rden"][:], sm["t3"][:]).then_inc(s_den, 1)
            v.memset(KR[0][64:128, :], 0.0)
            v.memset(KR[1][0:64, :], 0.0)
            lo("wa", 0, 0)
            dve.wait_ge(s_par, 16 * 2)
            for k in range(KD):
                dve.wait_ge(s_thi, k + 1)
                v.scalar_tensor_tensor(out=GL[:, k, :], in0=X[:, k, :], scalar=gain("mix0", k),
                                       in1=GH[:, k, :].bitcast(F32), op0=ALU.mult, op1=ALU.subtract).then_inc(s_act, 1)
                add_square("x", k, k % 2, first=(k == 0))
                if k == 3:
                    lo("wa", 0, 1)
            rstd("x", RSTD, RCOL)

            def latent(b):
                v.tensor_tensor(CR[b % 2][:], bank[b % 2][:], RSTD[:], ALU.mult).then_inc(s_ev, 1)

            def latent_lo(b):
                g = gain("q", b) if b < KQ else gain("kv", b - KQ)
                dve.wait_ge(s_thi, TILE0["c"] + b + 1)
                v.scalar_tensor_tensor(out=AL[:, b, :], in0=CR[b % 2][:], scalar=g, in1=AH[:, b, :].bitcast(F32),
                                       op0=ALU.mult, op1=ALU.subtract).then_inc(s_act, 1)
                add_square("c", b, b % 2, ss=SS if b < KQ else SSKV, first=b in (0, KQ))

            def rotate(k, dst):
                dve.wait_ge(s_pm, k + 1)
                v.tensor_tensor(TMP[:], bank[6 + k % 2][:], SIN[:], ALU.mult)
                v.tensor_tensor(RAWR[k % 2][:], RAWR[k % 2][:], COS[:], ALU.mult)
                v.drain()
                for rows, t in dst:
                    v.tensor_tensor(t, RAWR[k % 2][rows, :], TMP[rows, :], ALU.add)
                v.drain()

            for b in range(6):
                dve.wait_ge(s_mm, b + 1)
                lo_next("wa", b // 2, b % 2, b // 2 == 2)
                if b < 5:
                    latent(b)
                    latent_lo(b)
                if b == 4:
                    rstd("q", RSTDQ, RCOL)
                if b == 5:
                    v.tensor_tensor(RAWR[0][:], bank[1][:], RSTD[:], ALU.mult).then_inc(s_ev, 1)
                    dve.wait_ge(s_trig, 6)
                    rstd("kv", RSTDKV, RCKV)
                    rotate(0, [(slice(0, 64), KR[0][0:64, :]), (slice(64, 128), KR[1][64:128, :])])

            dve.wait_ge(s_tab, 16 * 3)
            for b in range(6):
                gb = FIRST["uq"] + b
                dve.wait_ge(s_mm, gb + 1)
                lo_next("uq", b // 2, b % 2, b // 2 == 2)
                for u in range(2):
                    src = bank[b % 2 + 4 * u][:]
                    if b < 2:
                        r = 2 * b + u
                        m = v.scalar_tensor_tensor(out=RAWR[(r + 1) % 2][:], in0=src, scalar=SCALE, in1=RSTDQ[:],
                                                   op0=ALU.mult, op1=ALU.mult)
                    else:
                        m = v.scalar_tensor_tensor(out=Qn[:, 2 * (b - 2) + u, :], in0=src, scalar=SCALE,
                                                   in1=RSTDQ[:], op0=ALU.mult, op1=ALU.mult)
                m.then_inc(s_ev, 1)
                if b < 2:
                    for u in range(2):
                        r = 2 * b + u
                        rotate(r + 1, [(slice(0, 128), QR[:, r, :])])
            for b in range(2):
                dve.wait_ge(s_mm, FIRST["uk"] + b + 1)
                lo_next("uk", 0, b, True)
                for u, bk in enumerate(KV_BANKS[b]):
                    m = v.tensor_tensor(Kn[:, 4 * b + u, :], bank[bk][:], RSTDKV[:], ALU.mult)
                m.then_inc(s_ev, 1)
            for b in range(2):
                dve.wait_ge(s_mm, FIRST["uv"] + b + 1)
                lo_next("uv", 0, b, True)
                for u, bk in enumerate(KV_BANKS[b]):
                    m = v.tensor_scalar(V[:, u, 512 * b:512 * b + 512], bank[bk][:], RCKV[:, u:u + 1], None, ALU.mult)
                m.then_inc(s_ev, 1)

            def row_max(n):
                qb = n % 4
                N = (qb + 1) * P
                dve.wait_ge(s_sc, n + 1)
                v.memset(bank[2 + qb][0:CHUNK, N - CHUNK:N], NEG)
                v.drain()
                v.tensor_reduce(MX[:, n:n + 1], bank[2 + qb][:, :N], AX.X, ALU.max, negate=True).then_inc(s_mx, 1)

            def normalize(n):
                qb = n % 4
                N = (qb + 1) * P
                dve.wait_ge(s_p, n + 1)
                v.reciprocal(RS[:, n:n + 1], SM[:, n:n + 1])
                v.drain()
                v.tensor_scalar(PR_[:, qb, :N], PR_[:, qb, :N], RS[:, n:n + 1], None, ALU.mult).then_inc(s_pn, 1)

            def o_lo(h):
                dve.wait_ge(s_thi, TILE0["o"] + h + 1)
                v.tensor_tensor(AL[:, h, :], bank[h % 2][:], AH[:, h, :].bitcast(F32), ALU.subtract).then_inc(s_act, 1)

            for n in range(4 * HEADS + 5):
                if n < 4 * HEADS:
                    row_max(n)
                if 1 <= n <= 4 * HEADS:
                    normalize(n - 1)
                if n >= 7 and n % 4 == 0:
                    o_lo((n - 8) // 4)
            for p in range(2):
                v.memset(Z[p][:, 0:2], 0.0)
            v.drain()

            def next_tile(key, kind, j, p, first=False):
                if kind != "final":
                    dve.wait_ge(s_thi, TILE0[key] + j + 1)
                    v.scalar_tensor_tensor(out=one(GL, j), in0=one(X, j), scalar=gain(kind, j),
                                           in1=one(GH, j).bitcast(F32), op0=ALU.mult, op1=ALU.subtract).then_inc(s_act, 1)
                add_square(key, j, p, first=first)

            def add_x(b, j, p):
                v.tensor_tensor(one(X, j), bank[p][:], one(X, j), ALU.add).then_inc(s_ev, 1)

            def wo(i, last):
                for p in range(2):
                    b = FIRST["wo"] + 2 * i + p
                    dve.wait_ge(s_mm, b + 1)
                    lo_next("wo", i, p, last)
                    add_x(b, 2 * i + p, p)
                    next_tile("n_wo", "ffn0", 2 * i + p, p, first=isinstance(i, int) and i == 0 and p == 0)
            pair_loop(dve, 4, wo)

            def ffn(l, done):
                rstd(done[0], RSTD, RCOL)
                for t, (f0, n) in enumerate(THIRDS):
                    name = f"up{l}{t}"
                    hk = f"h{l}{t}"
                    c0 = 2 * NF * l + 2 * f0

                    def tap(k, i, p):
                        if isinstance(i, int):
                            return CONV[:, c0 + 2 * i + p, k:k + 1]
                        return CONV[:, bass.ds(c0 + 2 * i + p, 1), k:k + 1].rearrange("p a b -> p (a b)")

                    def hidden(i):
                        dve.wait_ge(s_sg, NF * l + f0 + i + 1)
                        v.tensor_tensor(HH[:], SG[:], CV[0][:], ALU.mult).then_inc(s_h, 1)

                    def hidden_lo(i):
                        dve.wait_ge(s_thi, TILE0[hk] + i + 1)
                        v.tensor_tensor(one(AL, i), HH[:], one(AH, i).bitcast(F32), ALU.subtract).then_inc(s_act, 1)

                    def up(i, last):
                        first = isinstance(i, int) and i == 0
                        for p in range(2):
                            b = FIRST[name] + 2 * i + p
                            dve.wait_ge(s_mm, b + 1)
                            lo_next(name, i, p, last)
                            if p == 0 and not first:
                                hidden(i - 1)
                            v.tensor_tensor(Z[p][:, 2:S + 2], bank[p][:], RSTD[:], ALU.mult).then_inc(s_ev, 1)
                            if p == 0 and not first:
                                hidden_lo(i - 1)
                        for p in range(2):
                            dve.wait_ge(s_c, 2 * (NF * l + f0 + i) + p + 1)
                            v.scalar_tensor_tensor(out=CV[p][:], in0=Z[p][:, 1:S + 1], scalar=tap(1, i, p),
                                                   in1=CV[p][:], op0=ALU.mult, op1=ALU.add)
                            v.drain()
                            m = v.scalar_tensor_tensor(out=CV[p][:], in0=Z[p][:, 0:S], scalar=tap(0, i, p),
                                                       in1=CV[p][:], op0=ALU.mult, op1=ALU.add)
                        m.then_inc(s_cv, 1)
                    pair_loop(dve, n, up)
                    hidden(n - 1)
                    hidden_lo(n - 1)
                    dn = f"dn{l}{t}"

                    def down(i, last):
                        for p in range(2):
                            b = FIRST[dn] + 2 * i + p
                            dve.wait_ge(s_mm, b + 1)
                            lo_next(dn, i, p, last)
                            add_x(b, 2 * i + p, p)
                            if t == 2:
                                next_tile(done[1], done[2], 2 * i + p, p, first=isinstance(i, int) and i == 0 and p == 0)
                    pair_loop(dve, KD // 2, down)

            ffn(0, ("n_wo", "n_dn02", "mix1"))

            v.memset(ZERO[:], 0.0).then_inc(s_zz, 1)
            rstd("n_dn02", RSTD, RCOL)
            dve.wait_ge(s_kz, 128)
            for p in range(2):
                v.memset(XR[p][:, :, 0:1], 0.0)
                v.memset(XI[p][:, :, 0:1], 0.0)

            def u_out(j, p):
                if not (isinstance(j, int) and j == 0):
                    dve.wait_ge(s_uw, 16 * j)
                v.tensor_tensor(UB[:], bank[p][:].rearrange("p (k s) -> p s k", s=LQ),
                                RSTD[:].rearrange("p (k s) -> p s k", s=LQ), ALU.mult).then_inc(s_ev, 1)

            def matrices(j, p):
                dve.wait_ge(s_et, j + 1)
                if not (isinstance(j, int) and j < 2):
                    dve.wait_ge(s_E, j - 1)
                    dve.wait_ge(s_kw, 16 * (j - 1))
                for r in range(2):
                    v.tensor_copy(ET[p][:, r, :, :], bank[4 + r][:].rearrange("p (q m) -> p q m", q=4))
                dc = DCOL[:, 8 * j:8 * j + 8] if isinstance(j, int) else DCOL[:, bass.ds(8 * j, 8)]
                v.tensor_tensor(KALL[p][:], MASK[:].unsqueeze(1).broadcast_to([P, 8, C]),
                                dc.unsqueeze(2).broadcast_to([P, 8, C]), ALU.mult)
                v.drain()
                v.tensor_tensor(KALL[p][:], KALL[p][:], bank[3][:, 0:P].rearrange("p (g c) -> p g c", c=C),
                                ALU.add).then_inc(s_kall, 1)

            def cols(t, j):
                return t[:, 4 * j:4 * j + 4, :].rearrange("p q k -> p (q k)") if isinstance(j, int) else \
                    t[:, bass.ds(4 * j, 4), :].rearrange("p q k -> p (q k)")

            def states(j, p):
                n = 4 * NK
                dve.wait_ge(s_E, j + 1)
                er, ei = bank[2][:, 0:n], bank[2][:, n:2 * n]
                a, b_, c_, e, a2, c2 = (t[:] for t in R4)
                v.tensor_tensor(a, er, cols(WC, j), ALU.mult)
                v.tensor_tensor(b_, ei, cols(WS, j), ALU.mult)
                v.tensor_tensor(c_, ei, cols(WC, j), ALU.mult)
                v.tensor_tensor(e, er, cols(WS, j), ALU.mult)
                v.drain()
                v.tensor_tensor(a, a, b_, ALU.add)
                v.tensor_tensor(c_, c_, e, ALU.subtract)
                v.drain()
                v.tensor_tensor_scan(b_, cols(RT, j), a, 0.0, ALU.mult, ALU.add)
                v.tensor_tensor_scan(e, cols(RT, j), c_, 0.0, ALU.mult, ALU.add)
                v.drain()
                q = "p (q k) -> p q k"
                wc, ws = cols(WC, j).rearrange(q, k=NK), cols(WS, j).rearrange(q, k=NK)
                zr, zi = b_.rearrange(q, k=NK), e.rearrange(q, k=NK)
                t1, t2, t3, t4 = (t.rearrange(q, k=NK) for t in (a, c_, a2, c2))
                v.tensor_tensor(t1, zr, wc, ALU.mult)
                v.tensor_tensor(t2, zi, ws, ALU.mult)
                v.tensor_tensor(t3, zr, ws, ALU.mult)
                v.tensor_tensor(t4, zi, wc, ALU.mult)
                v.drain()
                v.tensor_tensor(XR[p][:, :, 1:], t1, t2, ALU.subtract)
                v.tensor_tensor(XI[p][:, :, 1:], t3, t4, ALU.add).then_inc(s_X, 1)

            def y_lo(j):
                dve.wait_ge(s_thi, TILE0["y"] + j + 1)
                t = "p (k s) -> p s k"
                v.tensor_tensor(one(AL, j).rearrange(t, s=LQ), YB[:], one(AH, j).bitcast(F32).rearrange(t, s=LQ),
                                ALU.subtract).then_inc(s_act, 1)

            def s5(i, last, first=False, tail=False):
                for p in range(2):
                    j = 2 * i + p
                    if not tail:
                        dve.wait_ge(s_mm, FIRST["win"] + j + 1)
                        lo_next("win", i, p, last)
                        u_out(j, p)
                        matrices(j, p)
                    if not (first and p == 0) and not (tail and p == 1):
                        states(j - 1, 1 - p)
                    if not first:
                        y_lo(j - 2)
            s5(0, False, first=True)
            with dve.Fori(1, 3) as i:
                s5(i, False)
            s5(3, True)
            s5(4, False, tail=True)

            def glu(i, last):
                first = isinstance(i, int) and i == 0
                for p in range(2):
                    b = FIRST["glu"] + 2 * i + p
                    dve.wait_ge(s_mm, b + 1)
                    lo_next("glu", i, p, last)
                    if p == 0:
                        v.tensor_copy(VAL[:], bank[0][:]).then_inc(s_ev, 1)
                v.drain()
                dve.wait_ge(s_sig, i + 1)
                v.tensor_tensor(VAL[:], VAL[:], SIG[:], ALU.mult)
                v.drain()
                v.tensor_tensor(one(X, i), VAL[:], one(X, i), ALU.add).then_inc(s_ev, 1)
                next_tile("n_glu", "ffn1", i, 0, first=first)
            pair_loop(dve, KD, glu)
            for p in range(2):
                v.memset(Z[p][:, 0:2], 0.0)
            v.drain()
            ffn(1, ("n_glu", "n_dn12", "final"))
            rstd("n_dn12", RSTD, RCOL)
            for k in range(KD):
                v.scalar_tensor_tensor(out=X[:, k, :], in0=X[:, k, :], scalar=gain("final", k), in1=RSTD[:],
                                       op0=ALU.mult, op1=ALU.mult).then_inc(s_fin, 1)

        @block.gpsimd
        def _(pool):
            g = nc.gpsimd
            sm = small

            def tt(out, a, b, op):
                return g.tensor_tensor(out, a, b, op)

            def cmul(o_r, o_i, ar, ai, br, bi, t1, t2, done=None):
                tt(t1, ar, br, ALU.mult)
                tt(t2, ai, bi, ALU.mult)
                g.drain()
                tt(o_r, t1, t2, ALU.subtract)
                g.drain()
                tt(t1, ar, bi, ALU.mult)
                tt(t2, ai, br, ALU.mult)
                g.drain()
                m = tt(o_i, t1, t2, ALU.add)
                if done is not None:
                    m.then_inc(done, 1)
                g.drain()

            f = {n: t[:] for n, t in small.items()}
            pool.wait_ge(s_trig, 6)
            pool.wait_ge(s_den, 1)
            tt(f["ar"], f["mag"], f["cs"], ALU.mult)
            tt(f["ai"], f["mag"], f["sn"], ALU.mult)
            g.drain()
            g.tensor_scalar(f["r"], f["ar"], -1.0, None, ALU.add)
            g.drain()
            tt(f["t1"], f["r"], f["lr"], ALU.mult)
            tt(f["t2"], f["ai"], f["li"], ALU.mult)
            g.drain()
            tt(f["t1"], f["t1"], f["t2"], ALU.add)
            g.drain()
            tt(f["cr"], f["t1"], f["rden"], ALU.mult)
            g.drain()
            tt(f["t1"], f["ai"], f["lr"], ALU.mult)
            tt(f["t2"], f["r"], f["li"], ALU.mult)
            g.drain()
            tt(f["t1"], f["t1"], f["t2"], ALU.subtract)
            g.drain()
            tt(f["ci"], f["t1"], f["rden"], ALU.mult)
            tt(f["r8"], f["mag"], f["mag"], ALU.mult)
            g.drain()
            for _ in range(2):
                tt(f["t1"], f["r8"], f["r8"], ALU.mult)
                g.drain()
                g.tensor_copy(f["r8"], f["t1"])
                g.drain()
            cmul(f["wr"], f["wi"], f["cs"], f["sn"], f["cs"], f["sn"], f["t1"], f["t2"])
            cmul(f["k"], f["th"], f["wr"], f["wi"], f["wr"], f["wi"], f["t1"], f["t2"])
            cmul(f["wr"], f["wi"], f["k"], f["th"], f["k"], f["th"], f["t1"], f["t2"])

            pool.wait_ge(s_mm, FIRST["wo"] + BLOCKS["wo"])
            g.memset(PWR[:, 0, :], 1.0)
            g.memset(PWI[:, 0, :], 0.0)
            g.drain()
            for k in range(LQ):
                cmul(PWR[:, k + 1, :], PWI[:, k + 1, :], PWR[:, k, :], PWI[:, k, :], f["ar"], f["ai"], f["t1"], f["t2"])
            g.memset(WC[:, :, 0:1], 1.0)
            g.memset(WS[:, :, 0:1], 0.0)
            g.drain()
            n = 1
            wk = ((f["wr"], f["wi"]), (f["k"], f["th"]))
            t1, t2 = PT1_[:], PT2_[:]
            while n < NK:
                (wr, wi), other = wk
                half = max(1, NQ * n // 512)
                nq = NQ // half
                for q0 in range(0, NQ, nq):
                    def bc(x):
                        return x[:, q0:q0 + nq].unsqueeze(2).broadcast_to([P, nq, n])

                    def tmp(t):
                        return t[:, 0:nq * n].rearrange("p (q k) -> p q k", k=n)
                    sl = slice(q0, q0 + nq)
                    cmul(WC[:, sl, n:2 * n], WS[:, sl, n:2 * n], WC[:, sl, 0:n], WS[:, sl, 0:n], bc(wr), bc(wi),
                         tmp(t1), tmp(t2))
                n *= 2
                if n < NK:
                    cmul(other[0], other[1], wr, wi, wr, wi, f["t1"], f["t2"])
                    wk = (other, (wr, wi))
            g.tensor_copy(RT[:], f["r8"].unsqueeze(2).broadcast_to([P, NQ, NK]))
            g.drain()
            g.memset(RT[:, :, 0:1], 0.0)
            pool.wait_ge(s_spar, 16 * 7)
            big = PT1_[:, 0:NQ * C].rearrange("p (q c) -> p q c", c=C)
            big2 = PT2_[:, 0:NQ * C].rearrange("p (q c) -> p q c", c=C)
            cmul(BBR[:], BBI[:], f["cr"].unsqueeze(2).broadcast_to([P, NQ, C]),
                 f["ci"].unsqueeze(2).broadcast_to([P, NQ, C]), BRE[:], BIM[:], big, big2)
            g.tensor_scalar(CIN[:], CIN[:], -1.0, None, ALU.mult)
            g.tensor_scalar(CBI[:], CBI[:], -1.0, None, ALU.mult)
            g.drain()

            def matrices(j, p):
                sh = [P, 4, LQ, C]

                def pw(t, m0):
                    x = t[:, m0:m0 + LQ, 4 * j:4 * j + 4] if isinstance(j, int) else t[:, m0:m0 + LQ, bass.ds(4 * j, 4)]
                    return x.rearrange("p m q -> p q m").unsqueeze(3).broadcast_to(sh)

                def ch(t):
                    x = t[:, 4 * j:4 * j + 4, :] if isinstance(j, int) else t[:, bass.ds(4 * j, 4), :]
                    return x.unsqueeze(2).broadcast_to(sh)
                a = PT1_[:].rearrange("p (q m c) -> p q m c", q=4, m=LQ)
                b_ = PT2_[:].rearrange("p (q m c) -> p q m c", q=4, m=LQ)
                if not (isinstance(j, int) and j == 0):
                    pool.wait_ge(s_et, j)
                cmul(GR[:], GI[:], pw(PWR, 0), pw(PWI, 0), ch(BBR), ch(BBI), a, b_, s_G)
                if not (isinstance(j, int) and j < 2):
                    pool.wait_ge(s_Y, j - 1)
                tt(a, pw(PWR, 1), ch(CRE), ALU.mult)
                tt(b_, pw(PWI, 1), ch(CIN), ALU.mult)
                g.drain()
                tt(OR[p][:], a, b_, ALU.add)
                g.drain()
                tt(a, pw(PWR, 1), ch(CIN), ALU.mult)
                tt(b_, pw(PWI, 1), ch(CRE), ALU.mult)
                g.drain()
                tt(OI[p][:], a, b_, ALU.subtract).then_inc(s_O, 1)
                g.drain()
            matrices(0, 0)
            matrices(1, 1)
            with pool.Fori(1, 4) as i:
                for p in range(2):
                    matrices(2 * i + p, p)

        @block.tensor
        def _(pe):
            mm = nc.tensor.matmul

            def unit(out, w, u, hi_, lo_, k, start, stop):
                wh, wl = WH[w][:, u * P:(u + 1) * P], WL[w][:, u * P:(u + 1) * P]
                mm(out, wh, hi_[:, k, :], start=start, stop=False)
                mm(out, wh, lo_[:, k, :], start=False, stop=False)
                return mm(out, wl, hi_[:, k, :], start=False, stop=stop)

            def ready(b):
                pe.wait_ge(s_lo, b + 1)
                if not (isinstance(b, int) and b < 2):
                    pe.wait_ge(s_ev, b - 1)

            def stats(norm, ss=None):
                ss = ss or SS
                pe.wait_ge(s_ss, SQ_END[norm])
                for t in range(TT):
                    m = mm(bank[2][:, t:t + 1], ss[:, t * P:(t + 1) * P], ONES[:, 0:1], start=True, stop=True)
                m.then_inc(s_st, 1)

            def bcast(norm):
                pe.wait_ge(s_dg, NORMS.index(norm) + 1)
                mm(bank[3][:], ONES[:], DIAG[:].rearrange("p a b -> p (a b)"), start=True, stop=True).then_inc(s_bc, 1)

            def first_pair(name, tile0, n, hi_, lo_, norm=None):
                B = FIRST[name]
                for p in range(2):
                    ready(B + p)
                    if name == "wo":
                        pe.wait_ge(s_act, tile0 + HEADS - 1 + p)
                    for k in range(n - 1):
                        if p == 0 and name != "wo":
                            pe.wait_ge(s_act, tile0 + k + 1)
                        unit(bank[p][:], p, k, hi_, lo_, k, k == 0, False)
                        if norm and p == 1 and k == n // 2:
                            stats(norm)
                if norm:
                    bcast(norm)
                pe.wait_ge(s_act, tile0 + n)
                for p in range(2):
                    unit(bank[p][:], p, n - 1, hi_, lo_, n - 1, False, True).then_inc(s_mm, 1)

            def other_pairs(name, n, hi_, lo_):
                def pair(i):
                    for p in range(2):
                        ready(FIRST[name] + 2 * i + p)
                        for k in range(n):
                            m = unit(bank[p][:], p, k, hi_, lo_, k, k == 0, k == n - 1)
                        m.then_inc(s_mm, 1)
                if BLOCKS[name] == 4:
                    pair(1)
                else:
                    with pe.Fori(1, BLOCKS[name] // 2) as i:
                        pair(i)

            pe.wait_ge(s_const, 1)
            first_pair("wa", TILE0["x"], KD, GH, GL, norm=None)
            stats("x")
            pe.wait_ge(s_tab, 16 * 3)
            bcast("x")
            for b in range(2, 6):
                ready(b)
                for k in range(KD):
                    m = unit(bank[b % 2][:], b % 2, k, GH, GL, k, k == 0, k == KD - 1)
                m.then_inc(s_mm, 1)
            stats("q")
            bcast("q")
            stats("kv", SSKV)
            bcast("kv")

            def permute(k):
                mm(bank[6 + k % 2][:], PERM[:], RAWR[k % 2][:], start=True, stop=True).then_inc(s_pm, 1)
            pe.wait_ge(s_ev, 6)
            permute(0)
            for b in range(6):
                B = FIRST["uq"] + b
                ready(B)
                if b == 0:
                    pe.wait_ge(s_act, TILE0["c"] + KQ)
                for u in range(2):
                    for k in range(KQ):
                        m = unit(bank[b % 2 + 4 * u][:], b % 2, KQ * u + k, AH, AL, k, k == 0, k == KQ - 1)
                m.then_inc(s_mm, 1)
                if b in (1, 2):
                    pe.wait_ge(s_ev, B)
                    permute(2 * b - 1)
                    permute(2 * b)
            for b in range(2):
                ready(FIRST["uk"] + b)
                if b == 0:
                    pe.wait_ge(s_act, TILE0["c"] + KQ + KKV)
                    pe.wait_ge(s_ev, FIRST["uk"])
                for u, bk in enumerate(KV_BANKS[b]):
                    for k in range(KKV):
                        m = unit(bank[bk][:], b, KKV * u + k, AH, AL, KQ + k, k == 0, k == KKV - 1)
                m.then_inc(s_mm, 1)
            for b in range(2):
                ready(FIRST["uv"] + b)
                for u, bk in enumerate(KV_BANKS[b]):
                    for k in range(KKV):
                        ts = slice(u * P, (u + 1) * P)
                        wh, wl = WH[b][:, 512 * k:512 * k + 512], WL[b][:, 512 * k:512 * k + 512]
                        mm(bank[bk][:], AH[:, KQ + k, ts], wh, start=(k == 0), stop=False)
                        mm(bank[bk][:], AH[:, KQ + k, ts], wl, start=False, stop=False)
                        m = mm(bank[bk][:], AL[:, KQ + k, ts], wh, start=False, stop=(k == KKV - 1))
                m.then_inc(s_mm, 1)

            def scores(n):
                h, qb = n // 4, n % 4
                N = (qb + 1) * P
                if n >= 4:
                    pe.wait_ge(s_p, n - 3)
                qs = slice(qb * P, (qb + 1) * P)
                mm(bank[2 + qb][:, :N], Qn[:, h, qs], Kn[:, h, :N], start=True, stop=False)
                mm(bank[2 + qb][:, :N], QR[:, h // 2, qs], KR[h % 2][:, :N], start=False, stop=True).then_inc(s_sc, 1)

            def turn(n):
                qb = n % 4
                pe.wait_ge(s_pn, n + 1)
                if n >= 2:
                    pe.wait_ge(s_ptc, n - 1)
                for kb in range(qb + 1):
                    m = nc.tensor.transpose(bank[6 + qb % 2][:, kb * P:(kb + 1) * P],
                                            PR_[:, qb, kb * P:(kb + 1) * P], IDENT[:])
                m.then_inc(s_pt, 1)

            def pv(h):
                pe.wait_ge(s_ptc, 4 * h + 4)
                if h >= 2:
                    pe.wait_ge(s_act, TILE0["o"] + h - 1)
                for kb in range(TT):
                    m = mm(bank[h % 2][:, kb * P:], V[:, kb, h * VH:(h + 1) * VH], PT[h % 2][:, kb, kb * P:],
                           start=(kb == 0), stop=(kb == TT - 1))
                m.then_inc(s_pv, 1)

            pe.wait_ge(s_ev, FIRST["wo"])
            for n in range(4 * HEADS + 4):
                if n < 4 * HEADS:
                    scores(n)
                if 2 <= n < 4 * HEADS + 2:
                    turn(n - 2)
                if n >= 7 and n % 4 == 3:
                    pv((n - 7) // 4)
            first_pair("wo", TILE0["o"], HEADS, AH, AL)
            other_pairs("wo", KD, AH, AL)

            def ffn(l, norm, tile0):
                for t, (f0, n) in enumerate(THIRDS):
                    first_pair(f"up{l}{t}", tile0, KD, GH, GL, norm=norm if t == 0 else None)
                    other_pairs(f"up{l}{t}", KD, GH, GL)
                    first_pair(f"dn{l}{t}", TILE0[f"h{l}{t}"], n, AH, AL)
                    other_pairs(f"dn{l}{t}", n, AH, AL)
            ffn(0, "n_wo", TILE0["n_wo"])

            def matrices(j, p):
                pe.wait_ge(s_G, j + 1)
                if isinstance(j, int) and j == 0:
                    pe.wait_ge(s_rstd, NORMS.index("n_dn02") + 1)
                if not (isinstance(j, int) and j == 0):
                    pe.wait_ge(s_kall, j)
                for r, src in enumerate((GR, GI)):
                    for q in range(4):
                        nc.tensor.transpose(bank[4 + r][:, q * P:(q + 1) * P],
                                            src[:, q, :, :].rearrange("p m c -> p (m c)"), IDENT[:])
                for q in range(4):
                    cs = slice(q * 2 * C, (q + 1) * 2 * C)
                    c = [t[:, 4 * j + q, :] if isinstance(j, int) else
                         t[:, bass.ds(4 * j + q, 1), :].rearrange("p a c -> p (a c)") for t in (CBR, CBI)]
                    mm(bank[3][:, cs], GR[:, q, :, :].rearrange("p m c -> p (m c)"), c[0], start=True, stop=False)
                    m = mm(bank[3][:, cs], GI[:, q, :, :].rearrange("p m c -> p (m c)"), c[1], start=False, stop=True)
                m.then_inc(s_et, 1)

            def s5(i, last, first=False, tail=False):
                for p in range(2):
                    j = 2 * i + p
                    if not tail:
                        if not first:
                            ready(FIRST["win"] + j)
                            for k in range(KD):
                                m = unit(bank[p][:], p, k, GH, GL, k, k == 0, k == KD - 1)
                            m.then_inc(s_mm, 1)
                        matrices(j, p)
                    if not (first and p == 0) and not (tail and p == 1):
                        q_ = 1 - p
                        pe.wait_ge(s_ur[q_], 128 * (i + p))
                        pe.wait_ge(s_kall, j)
                        if not (isinstance(j, int) and j == 1):
                            pe.wait_ge(s_X, j - 1)
                        for q in range(4):
                            for r in range(2):
                                for gi in range(2):
                                    rows = slice(64 * gi, 64 * gi + 64)
                                    c0 = (4 * r + q) * NK
                                    m = mm(bank[2][rows, c0:c0 + NK], ET[q_][:, r, q, rows], U2[q_][:, 2 * q + gi, :],
                                           start=True, stop=True)
                        m.then_inc(s_E, 1)
                    if not first:
                        pe.wait_ge(s_X, j - 1)
                        pe.wait_ge(s_tm, j - 1)
                        pe.wait_ge(s_O, j - 1)
                        if not (isinstance(j, int) and j == 2):
                            pe.wait_ge(s_g, j - 2)
                        for q in range(4):
                            for gi in range(2):
                                rows = slice(64 * gi, 64 * gi + 64)
                                gg = 2 * q + gi
                                out = bank[6 + gi][:, q * NK:(q + 1) * NK]
                                mm(out, TM[p][:, gg, :, :].rearrange("p s c -> p (s c)"), U2[p][:, gg, :], start=True, stop=False)
                                mm(out, OR[p][rows, q, :, :].rearrange("p m c -> p (m c)"), XR[p][rows, q, 0:NK],
                                   start=False, stop=False)
                                m = mm(out, OI[p][rows, q, :, :].rearrange("p m c -> p (m c)"), XI[p][rows, q, 0:NK],
                                       start=False, stop=True)
                        m.then_inc(s_Y, 1)
            first_pair("win", TILE0["n_dn02"], KD, GH, GL, norm="n_dn02")
            s5(0, False, first=True)
            with pe.Fori(1, 3) as i:
                s5(i, False)
            s5(3, True)
            s5(4, False, tail=True)
            first_pair("glu", TILE0["y"], KD, AH, AL)
            other_pairs("glu", KD, AH, AL)
            ffn(1, "n_glu", TILE0["n_glu"])
            stats("n_dn12")
            bcast("n_dn12")


KV_BANKS = ((0, 4, 6, 2), (1, 5, 7, 3))


def kernel(**inp):
    import concourse.bacc as bacc
    from concourse.bass_utils import run_bass_kernel_spmd as run

    a = {k: np.asarray(v) for k, v in inp.items()}
    arrays = {}

    def put(name, x):
        arrays[name] = np.ascontiguousarray(x)

    def blocks(w, n=P):
        k, m = w.shape
        return w.reshape(k // P, P, m // n, n).transpose(2, 1, 0, 3).reshape(m // n, P, k // P * n)

    def halves(x):
        x = x.reshape((NQ, 2, PS) + x.shape[2:])
        return np.moveaxis(x, 0, 2).reshape((2 * PS, NQ) + x.shape[3:])

    put("x", a["x"][0].T.reshape(KD, P, S))
    put("pos", a["positions"][0])
    put("inv", np.tile((1.0 / (np.float32(THETA) ** (np.arange(0, ROPE, 2, dtype=np.float32) / np.float32(ROPE)))
                        ).astype(np.float32), 4)[:, None])
    cols = lambda g: g.reshape(-1, P).T
    put("gain", np.concatenate([cols(a["g_mix"][0]), cols(a["g_mix"][1]), cols(a["g_ffn"][0]), cols(a["g_ffn"][1]),
                                cols(a["g_final"]), cols(a["mla_g_q"][0]), cols(a["mla_g_kv"][0])], axis=1))
    put("ident", np.eye(P, dtype=np.float32))
    perm = np.zeros((P, P), np.float32)
    for r in range(P):
        o = r % 64
        perm[r + 32 if o < 32 else r - 32, r] = -1.0 if o < 32 else 1.0
    put("perm", perm)
    cw = np.concatenate([a["ffn_conv_w"], a["ffn_conv_b"][:, None, :]], axis=1)
    put("conv", cw.reshape(DEPTH, 4, 2, NF, P).transpose(4, 0, 3, 2, 1).reshape(P, DEPTH * 2 * NF, 4))

    wa = a["mla_w_a"][0]
    kr = wa[:, Q_LORA + KV_LORA:]
    put("w_wa", blocks(np.concatenate([wa[:, :Q_LORA + KV_LORA], kr, kr], axis=1)))
    uq = a["mla_w_uq"][0].reshape(Q_LORA, HEADS, NOPE + ROPE)
    uq = np.concatenate([uq[:, :, NOPE:].reshape(Q_LORA, HEADS * ROPE), uq[:, :, :NOPE].reshape(Q_LORA, HEADS * NOPE)], 1)
    put("w_uq", blocks(uq).reshape(6, 2, P, KQ * P).transpose(0, 2, 1, 3).reshape(6, P, 2 * KQ * P))
    ukv = a["mla_w_ukv"][0].reshape(KV_LORA, HEADS, NOPE + VH)
    put("w_uk", blocks(ukv[:, :, :NOPE].reshape(KV_LORA, HEADS * NOPE)).reshape(2, 4, P, KKV * P)
        .transpose(0, 2, 1, 3).reshape(2, P, 8 * P))
    put("w_uv", blocks(ukv[:, :, NOPE:].reshape(KV_LORA, HEADS * VH), 512))
    put("w_wo", blocks(a["mla_w_o"][0]))
    put("w_win", blocks(a["ssm_w_in"][0]))
    glu = a["ssm_w_glu"][0].reshape(D, 2, KD, P).transpose(0, 2, 1, 3).reshape(D, 2 * D)
    put("w_glu", blocks(glu))
    for l in range(DEPTH):
        up = a["ffn_w_up"][l].reshape(D, 2, NF, P).transpose(0, 2, 1, 3)
        for t, (f0, n) in enumerate(THIRDS):
            put(f"w_up{l}{t}", blocks(up[:, f0:f0 + n].reshape(D, 2 * n * P)))
            put(f"w_dn{l}{t}", blocks(a["ffn_w_down"][l][f0 * P:(f0 + n) * P]))

    put("lr", halves(a["ssm_lambda_re"][0]))
    put("li", halves(a["ssm_lambda_im"][0]))
    put("ld", halves(np.broadcast_to(a["ssm_log_dt"][0][:, None], (G, PS))))
    put("bre", halves(a["ssm_b_re"][0]))
    put("bim", halves(a["ssm_b_im"][0]))
    for n, src in (("re", "ssm_c_re"), ("im", "ssm_c_im")):
        c = halves(a[src][0].transpose(0, 2, 1))
        put("c" + n, c)
        bd = np.zeros((P, NQ, 2 * C), np.float32)
        bd[:PS, :, :C] = c[:PS]
        bd[PS:, :, C:] = c[PS:]
        put("cb" + n[0], bd)
    dcol = np.zeros((P, G), np.float32)
    dcol[:C] = a["ssm_d"][0].reshape(G, C).T
    put("dcol", dcol)
    mask = np.zeros((P, C), np.float32)
    mask[:C] = np.eye(C, dtype=np.float32)
    put("mask", mask)

    nc = bacc.Bacc("TRN2", target_bir_lowering=False, num_devices=1, dynamic_dma_scratch_size=1024)
    d = {}
    for name, x in arrays.items():
        d[name] = nc.dram_tensor("in_" + name, x.shape, mybir.dt.from_np(x.dtype), kind="ExternalInput").ap()
    d["out"] = nc.dram_tensor("out", (KD, P, S), F32, kind="ExternalOutput").ap()
    build(nc, d)
    r = run(nc, [{"in_" + n: x for n, x in arrays.items()}], core_ids=[0])
    return np.ascontiguousarray(np.asarray(r.results[0]["out"]).reshape(D, S).T)[None]
```

```python
from contextlib import ExitStack

import numpy as np
import concourse.bass as bass
from concourse import mybir

P = 128
D, S, DEPTH = 1024, 512, 2
KD = D // P
TT = S // P
EPS = 1e-6
CHUNK = 64
HEADS, NOPE, ROPE, VH = 8, 128, 64, 128
Q_LORA, KV_LORA = 384, 256
KQ, KKV = Q_LORA // P, KV_LORA // P
SCALE = float(NOPE + ROPE) ** -0.5
THETA = 10000.0
D_FF = 2816
NF = D_FF // P
THIRDS = [(0, 8), (8, 8), (16, 6)]
G, PS, C = 64, 64, 16
NQ = G // 2
LQ = S // 64
NK = S // LQ
TWO_PI = 2.0 * np.pi
MAGIC = 12582912.0
PI_1 = 6.28125
PI_2 = float(np.float32(1.9350051879882812e-03))
PI_3 = float(TWO_PI - PI_1 - PI_2)
PI_IN = 3.1415925
NEG = -3.0e38

ALU = mybir.AluOpType
ACT = mybir.ActivationFunctionType
AX = mybir.AxisListType
F32 = mybir.dt.float32
FR = mybir.dt.float32r
I32 = mybir.dt.int32

PHASES = [("wa", 6, 8), ("uq", 6, 6), ("uk", 2, 8), ("uv", 2, 8), ("wo", 8, 8)]
for _l in range(DEPTH):
    if _l == 1:
        PHASES += [("win", 8, 8), ("glu", 16, 8)]
    for _t, (_f0, _n) in enumerate(THIRDS):
        PHASES += [(f"up{_l}{_t}", 2 * _n, 8), (f"dn{_l}{_t}", KD, _n)]
ORDER = [n for n, _, _ in PHASES]
BLOCKS = {n: b for n, b, _ in PHASES}
UNITS = {n: u for n, _, u in PHASES}
FIRST = {}
_b = 0
for _n, _c, _u in PHASES:
    FIRST[_n] = _b
    _b += _c
NBLOCKS = _b

TILE0, SQ0 = {}, {}
_b = 0
for _n, _c in [("x", 8), ("c", 5), ("o", 8), ("n_wo", 8), ("h00", 8), ("h01", 8), ("h02", 6), ("n_dn02", 8),
               ("y", 8), ("n_glu", 8), ("h10", 8), ("h11", 8), ("h12", 6)]:
    TILE0[_n] = _b
    _b += _c
_b = 0
for _n, _c in [("x", 8), ("c", 5), ("n_wo", 8), ("n_dn02", 8), ("n_glu", 8), ("n_dn12", 8)]:
    SQ0[_n] = _b
    _b += _c
NORMS = ["x", "q", "kv", "n_wo", "n_dn02", "n_glu", "n_dn12"]
SQ_END = {"x": 8, "q": 8 + KQ, "kv": 13, "n_wo": 21, "n_dn02": 29, "n_glu": 37, "n_dn12": 45}
WIDTH = {"q": Q_LORA, "kv": KV_LORA}


def following(name):
    n = ORDER.index(name) + 1
    return ORDER[n] if n < len(ORDER) else None


def pair_loop(eng, pairs, body):
    body(0, pairs == 1)
    if pairs > 2:
        with eng.Fori(1, pairs - 1) as i:
            body(i, False)
    if pairs > 1:
        body(pairs - 1, True)


def since(j, k):
    return not isinstance(j, int) or j >= k


def upto(j, k):
    return not isinstance(j, int) or j <= k


def s5_loop(eng, step):
    for j in range(4):
        step(j // 2, j % 2)
    with eng.Fori(2, 4) as i:
        for p in range(2):
            step(i, p)
    for j in range(8, 11):
        step(j // 2, j % 2)


def build(nc, d):
    ctx = ExitStack()
    with ctx:
        base = [(nc.sbuf_base + 63) // 64 * 64]

        def place(name, shape, dt, at):
            size = 4 * int(np.prod(shape[1:]))
            assert at + size <= nc.sbuf_usable_end, (name, at + size - nc.sbuf_usable_end)
            t = nc.alloc_sbuf_tensor_at(name, list(shape), dt, offset=at)
            return t, (at + size + 31) // 32 * 32

        def keep(name, shape, dt=F32):
            t, base[0] = place(name, shape, dt, base[0])
            return t

        def sem(name):
            return ctx.enter_context(nc.semaphore(name))

        X = keep("X", [P, KD, S])
        GH = keep("GH", [P, KD, S], FR)
        GL = keep("GL", [P, KD, S], FR)
        AH = keep("AH", [P, KD, S], FR)
        AL = keep("AL", [P, KD, S], FR)
        RAW = [keep(f"RAW{i}", [P, 8 * P]) for i in range(2)]
        WH = [keep(f"WH{i}", [P, 8 * P], FR) for i in range(2)]
        WL = [keep(f"WL{i}", [P, 8 * P], FR) for i in range(2)]
        RSTD = keep("RSTD", [P, S])
        SS = keep("SS", [P, S])
        SQ = [keep(f"SQ{i}", [P, S]) for i in range(2)]
        DIAG = keep("DIAG", [P, TT, P])
        IDENT = keep("IDENT", [P, P])
        PERM = keep("PERM", [P, P])
        ONES = keep("ONES", [P, P])
        GAIN = keep("GAIN", [P, 5 * KD + KQ + KKV])
        CONV = keep("CONV", [P, DEPTH * 2 * NF, 4])
        STD = keep("STD", [P, TT])
        RCOL = keep("RCOL", [P, TT])
        RCKV = keep("RCKV", [P, TT])
        EPST = keep("EPST", [P, 1])
        INV = keep("INV", [P, 1])
        MX = keep("MX", [P, 32])
        SM = keep("SM", [P, 32])
        RS = keep("RS", [P, 32])
        DCOL = keep("DCOL", [P, G])
        small = {n: keep("s_" + n, [P, NQ]) for n in
                 ("lr", "li", "ld", "dt", "ldt", "th", "mag", "sn", "cs", "k", "r", "rden", "ar", "ai", "cr", "ci",
                  "wr", "wi", "r8", "t1", "t2", "t3")}
        A0 = base[0]

        Qn, at = place("Qn", [P, HEADS, S], F32, A0)
        Kn, at = place("Kn", [P, HEADS, S], F32, at)
        QR, at = place("QR", [P, HEADS // 2, S], F32, at)
        KR = [None, None]
        KR[0], at = place("KR0", [P, S], F32, at)
        KR[1], at = place("KR1", [P, S], F32, at)
        V, at = place("V", [P, TT, HEADS * VH], F32, at)
        attn_b = at
        COS, at = place("COS", [P, S], F32, attn_b)
        SIN, at = place("SIN", [P, S], F32, at)
        CR = [None, None]
        CR[0], at = place("CR0", [P, S], F32, at)
        CR[1], at = place("CR1", [P, S], F32, at)
        RAWR = [None] * 4
        for i in range(4):
            RAWR[i], at = place(f"RAWR{i}", [P, S], F32, at)
        TMP, at = place("TMP", [P, S], F32, at)
        RSTDQ, at = place("RSTDQ", [P, S], F32, at)
        RSTDKV, at = place("RSTDKV", [P, S], F32, at)
        SSKV, at = place("SSKV", [P, S], F32, at)
        POSI, _ = place("POSI", [P, S], I32, A0)
        POSF, _ = place("POSF", [P, S], F32, A0 + 2048)
        KANG, _ = place("KANG", [P, S], F32, A0 + 4096)
        KTMP, _ = place("KTMP", [P, S], F32, A0 + 6144)
        PR_, at = place("Pexp", [P, TT, S], F32, attn_b)
        PT0, at = place("PT0", [P, TT, S], F32, at)
        PT1, at = place("PT1", [P, TT, S], F32, at)
        PT = [PT0, PT1]

        PWR, at = place("PWR", [P, LQ + 1, NQ], F32, A0)
        PWI, at = place("PWI", [P, LQ + 1, NQ], F32, at)
        WC, at = place("WC", [P, NQ, NK], F32, at)
        WS, at = place("WS", [P, NQ, NK], F32, at)
        RT, at = place("RT", [P, NQ, NK], F32, at)
        CRE, at = place("CRE", [P, NQ, C], F32, at)
        CIN, at = place("CIN", [P, NQ, C], F32, at)
        BBR, at = place("BBR", [P, NQ, C], F32, at)
        BBI, at = place("BBI", [P, NQ, C], F32, at)
        CBR, at = place("CBR", [P, NQ, 2 * C], F32, at)
        CBI, at = place("CBI", [P, NQ, 2 * C], F32, at)
        GR, at = place("GR", [P, 4, LQ, C], F32, at)
        GI, at = place("GI", [P, 4, LQ, C], F32, at)
        PT1_, at = place("PT1_", [P, 4 * LQ * C], F32, at)
        PT2_, at = place("PT2_", [P, 4 * LQ * C], F32, at)
        OO, OR, OI, ET, TM, KALL = ([None, None] for _ in range(6))
        ring0 = at
        for i in range(2):
            OO[i], at = place(f"OO{i}", [P, 2, 4 * LQ * C], F32, at)
            OR[i], OI[i] = (OO[i][:, r_, :].rearrange("p (q m c) -> p q m c", q=4, m=LQ) for r_ in range(2))
            ET[i], at = place(f"ET{i}", [P, 2, 4, P], F32, at)
            KALL[i], at = place(f"KALL{i}", [P, 8, C], F32, at)
        BRE, _ = place("BRE", [P, NQ, C], F32, ring0)
        BIM, _ = place("BIM", [P, NQ, C], F32, ring0 + 2048)
        MASK, at = place("MASK", [P, C], F32, at)
        f0 = at
        Z, CV = [None, None], [None, None]
        for i in range(2):
            Z[i], at = place(f"Z{i}", [P, S + 2], F32, at)
            CV[i], at = place(f"CV{i}", [P, S], F32, at)
        SG, at = place("SG", [P, S], F32, at)
        HH, at = place("HH", [P, S], F32, at)
        UB, U2, Y2, YB, XR, XI = ([None, None] for _ in range(6))
        at = f0
        for i in range(2):
            U2[i], at = place(f"U2{i}", [P, 8, NK], F32, at)
            XR[i], at = place(f"XR{i}", [P, 4, NK + 1], F32, at)
            XI[i], at = place(f"XI{i}", [P, 4, NK + 1], F32, at)
        for i in range(2):
            TM[i], at = place(f"TM{i}", [P, 8, LQ, C], F32, at)
        TMR, at = place("TMR", [P, LQ, 8, C], F32, at)
        UB, at = place("UB", [P, LQ, NK], F32, at)
        Y2, at = place("Y2", [P, 8, NK], F32, at)
        YB, at = place("YB", [P, LQ, NK], F32, at)
        R4 = []
        for i in range(6):
            t, at = place(f"R4{i}", [P, 4 * NK], F32, at)
            R4.append(t)
        VAL, _ = place("VAL", [P, S], F32, f0)
        SIG, _ = place("SIG", [P, S], F32, f0 + 2048)
        ZERO, _ = place("ZERO", [112, P], F32, f0)

        bank = [ctx.enter_context(nc.psum_tensor(f"bank{i}", [P, S], F32)) for i in range(8)]

        OD = nc.dram_tensor("od_scratch", (8, P, 2, 4 * LQ * C), F32, kind="Internal").ap()
        UD = nc.dram_tensor("ud_scratch", (8, P, LQ, NK), F32, kind="Internal").ap()
        YD = nc.dram_tensor("yd_scratch", (8, P, 8, NK), F32, kind="Internal").ap()
        KDR = nc.dram_tensor("kd_scratch", (8, 15 * C, P), F32, kind="Internal").ap()

        s_raw = [sem("raw0_loaded"), sem("raw1_loaded")]
        s_hi, s_lo, s_mm, s_ev = sem("w_hi"), sem("w_lo"), sem("block_done"), sem("bank_read")
        s_thi, s_act = sem("tile_hi"), sem("tile_lo")
        s_sq, s_ss = sem("squared"), sem("sq_summed")
        s_st, s_std, s_dg, s_bc, s_rstd = sem("stat"), sem("std"), sem("diag"), sem("bcast"), sem("rstd")
        s_x = [sem(f"x{k}_loaded") for k in range(KD)]
        s_par, s_tab, s_pos, s_const = sem("gain_loaded"), sem("tables_loaded"), sem("pos_loaded"), sem("const_made")
        s_ang, s_trig = sem("angles"), sem("trig")
        s_den = sem("ssm_den")
        s_pm, s_rot = sem("permuted"), sem("rotated")
        s_sc, s_mx, s_p, s_pn, s_pt, s_ptc, s_pv, s_oc = (sem(n) for n in (
            "scores", "row_max", "exps", "probs", "probs_t", "probs_t_copied", "pv", "o_read"))
        s_z, s_c, s_cv, s_sg, s_h = (sem(n) for n in ("z", "tap2", "conv", "gate", "hidden"))
        s_spar, s_zz, s_kz = sem("s5_loaded"), sem("zero_made"), sem("kd_zeroed")
        s_G, s_O, s_et, s_etc, s_kall = sem("G"), sem("O"), sem("ET"), sem("ET_copied"), sem("kall")
        s_ow, s_or = [sem("O0_written"), sem("O1_written")], [sem("O0_loaded"), sem("O1_loaded")]
        s_kw, s_T, s_tm = sem("kd_written"), sem("TMR_loaded"), sem("lags_sorted")
        s_u, s_uw, s_ur = sem("u"), sem("ud_written"), [sem("U0_loaded"), sem("U1_loaded")]
        s_E, s_X, s_Y, s_g = sem("E"), sem("states"), sem("Y"), sem("gelu")
        s_yw, s_yr = sem("yd_written"), sem("YB_loaded")
        s_val, s_sig = sem("val"), sem("sigmoid")
        s_fin, s_out = sem("final"), sem("out_written")

        block = ctx.enter_context(nc.Block())

        def gain(kind, k):
            g0 = {"mix0": 0, "mix1": KD, "ffn0": 2 * KD, "ffn1": 3 * KD, "final": 4 * KD,
                  "q": 5 * KD, "kv": 5 * KD + KQ}[kind]
            if isinstance(k, int):
                return GAIN[:, g0 + k:g0 + k + 1]
            return GAIN[:, bass.ds(g0 + k, 1)]

        def one(t, k):
            if isinstance(k, int):
                return t[:, k, :]
            return t[:, bass.ds(k, 1), :].rearrange("p a s -> p (a s)")

        @block.sync
        def _(sp):
            def load(name, i, p):
                b = FIRST[name] + 2 * i + p
                n = UNITS[name] * P
                if not (isinstance(b, int) and b < 2):
                    sp.wait_ge(s_lo, b - 1)
                src = d["w_" + name]
                sp.dma_start(RAW[p][:, :n], src[2 * i + p] if isinstance(i, int) else
                             src[bass.ds(2 * i + p, 1)].rearrange("a p n -> (a p) n")).then_inc(s_raw[p], 16)

            def load_next(name, i, p, last):
                if not last:
                    load(name, i + 1, p)
                elif following(name):
                    load(following(name), 0, p)

            sp.dma_start(POSI[:], d["pos"].partition_broadcast(P)).then_inc(s_pos, 16)
            sp.dma_start(INV[:], d["inv"]).then_inc(s_pos, 16)
            for n in ("lr", "li", "ld"):
                sp.dma_start(small[n][:], d[n]).then_inc(s_pos, 16)
            load("wa", 0, 0)
            for k in range(KD):
                sp.dma_start(X[:, k, :], d["x"][k]).then_inc(s_x[k], 16)
                if k == 1:
                    sp.dma_start(GAIN[:], d["gain"]).then_inc(s_par, 16)
                    sp.dma_start(IDENT[:], d["ident"]).then_inc(s_par, 16)
                if k == 3:
                    load("wa", 0, 1)
            sp.dma_start(PERM[:], d["perm"]).then_inc(s_tab, 16)
            sp.dma_start(CONV[:], d["conv"]).then_inc(s_tab, 16)
            sp.dma_start(DCOL[:], d["dcol"]).then_inc(s_tab, 16)

            def s5_params():
                sp.wait_ge(s_mm, FIRST["wo"] + BLOCKS["wo"])
                for t, n in ((BRE, "bre"), (BIM, "bim"), (CRE, "cre"), (CIN, "cim"), (CBR, "cbr"), (CBI, "cbi"),
                             (MASK, "mask")):
                    sp.dma_start(t[:], d[n]).then_inc(s_spar, 16)

            def s5_step(j):
                p = j % 2
                lag, y, u = 1 <= j <= 8, 3 <= j, j < 8
                if lag:
                    sp.wait_ge(s_kall, j)
                    sp.dma_start(KDR[j - 1][7 * C:15 * C, :], KALL[1 - p][:]).then_inc(s_kw, 16)
                if y:
                    sp.wait_ge(s_g, j - 2)
                    sp.dma_start(YD[j - 3], Y2[:]).then_inc(s_yw, 16)
                if lag:
                    sp.wait_ge(s_kw, 16 * j)
                    if j > 1:
                        sp.wait_ge(s_tm, j - 1)
                    k = KDR[j - 1]
                    sp.dma_start(TMR[:].rearrange("p s g c -> p s (g c)"),
                                 bass.AP(k.tensor, k.offset, [[P, P], [C * P, LQ], [1, P]])).then_inc(s_T, 16)
                if y:
                    sp.wait_ge(s_yw, 16 * (j - 2))
                    if j > 3:
                        sp.wait_ge(s_act, TILE0["y"] + j - 3)
                    for g in range(8):
                        sp.dma_start(YB[C * g:C * g + C], YD[j - 3].rearrange("(s c) g k -> g c s k", s=LQ)[g]
                                     ).then_inc(s_yr, 16)
                if u:
                    sp.wait_ge(s_ev, FIRST["win"] + j + 1)
                    sp.dma_start(UD[j], UB[:]).then_inc(s_uw, 16)
                    if j > 1:
                        sp.wait_ge(s_Y, j - 1)
                    sp.wait_ge(s_ow[p], 16 * (j // 2 + 1))
                    if j < 2:
                        sp.wait_ge(s_ow[p], 16 * 4)
                    sp.dma_start(OO[p][:], OD[j]).then_inc(s_or[p], 16)
                    sp.wait_ge(s_uw, 16 * (j + 1))
                    for s in range(LQ):
                        sp.dma_start(U2[p][C * s:C * s + C], UD[j].rearrange("(g c) s k -> s c g k", g=8)[
                            LQ - 1 - s]).then_inc(s_ur[p], 16)

            for name in ORDER:
                if name == "win":
                    sp.wait_ge(s_zz, 1)
                    for j in range(8):
                        sp.dma_start(KDR[j][0:7 * C, :], ZERO[:]).then_inc(s_kz, 16)
                    sp.wait_ge(s_kz, 128)

                    for j in range(11):
                        if j < 8:
                            load_next(name, j // 2, j % 2, j >= 6)
                        s5_step(j)
                    continue
                if name == "up00":
                    s5_params()
                pair_loop(sp, BLOCKS[name] // 2, lambda i, last: [load_next(name, i, p, last) for p in range(2)])
            for k in range(KD):
                sp.wait_ge(s_fin, k + 1)
                sp.dma_start(d["out"][k], X[:, k, :]).then_inc(s_out, 16)
            sp.wait_ge(s_out, 16 * KD)

        @block.scalar
        def _(act):
            act_ = nc.scalar.activation

            def hi(name, i, p):
                b = FIRST[name] + 2 * i + p
                n = UNITS[name] * P
                act.wait_ge(s_raw[p], 16 * (FIRST[name] // 2 + i + 1))
                if not (isinstance(b, int) and b < 2):
                    act.wait_ge(s_mm, b - 1)
                act_(WH[p][:, :n], RAW[p][:, :n], ACT.Copy).then_inc(s_hi, 1)

            def hi_next(name, i, p, last):
                if not last:
                    hi(name, i + 1, p)
                elif following(name):
                    hi(following(name), 0, p)

            def square(src, dst, key, j, p):
                if key in ("x", "c") and j >= 2:
                    act.wait_ge(s_ss, SQ0[key] + j - 1)
                act_(dst[:], src, ACT.Square).then_inc(s_sq, 1)

            def std(norm):
                act.wait_ge(s_st, NORMS.index(norm) + 1)
                act_(STD[:], bank[2][:, 0:TT], ACT.Sqrt, bias=EPST[:, 0:1],
                     scale=1.0 / WIDTH.get(norm, D)).then_inc(s_std, 1)

            hi("wa", 0, 0)
            act.wait_ge(s_par, 16 * 2)
            for k in range(KD):
                act.wait_ge(s_x[k], 16)
                act_(GH[:, k, :], X[:, k, :], ACT.Identity, scale=gain("mix0", k)).then_inc(s_thi, 1)
                square(X[:, k, :], SQ[k % 2], "x", k, k % 2)
                if k == 3:
                    hi("wa", 0, 1)
            act.wait_ge(s_const, 1)
            sm = small
            act.wait_ge(s_pos, 16 * 5)
            act_(sm["dt"][:], sm["ld"][:], ACT.Exp).then_inc(s_trig, 1)
            std("x")

            for b in range(6):
                act.wait_ge(s_mm, b + 1)
                hi_next("wa", b // 2, b % 2, b // 2 == 2)
                if b < 5:
                    act.wait_ge(s_ev, b + 1)
                    g = gain("q", b) if b < KQ else gain("kv", b - KQ)
                    act_(AH[:, b, :], CR[b % 2][:], ACT.Identity, scale=g).then_inc(s_thi, 1)
                    square(CR[b % 2][:], SQ[b % 2], "c", b, b % 2)
                if b == 3:
                    std("q")
                if b == 4:
                    act.wait_ge(s_ang, 1)
                    act_(sm["mag"][:], sm["ldt"][:], ACT.Exp).then_inc(s_trig, 1)
                if b == 5:
                    std("kv")
            for n, t in enumerate((COS, SIN)):
                act.wait_ge(s_ang, n + 2)
                act_(t[:], t[:], ACT.Sin).then_inc(s_trig, 1)
            act.wait_ge(s_tab, 16 * 3)
            for name in ("uq", "uk", "uv"):
                for b in range(BLOCKS[name]):
                    act.wait_ge(s_mm, FIRST[name] + b + 1)
                    hi_next(name, b // 2, b % 2, b // 2 == BLOCKS[name] // 2 - 1)
                    if name == "uq" and b == 0:
                        for n, t in enumerate((sm["cs"], sm["sn"])):
                            act.wait_ge(s_ang, n + 4)
                            act_(t[:], t[:], ACT.Sin).then_inc(s_trig, 1)

            def exps(n):
                qb = n % 4
                N = (qb + 1) * P
                act.wait_ge(s_mx, n + 1)
                if n >= 4:
                    act.wait_ge(s_pt, n - 3)
                act_(PR_[:, qb, :N], bank[2 + qb][:, :N], ACT.Exp, bias=MX[:, n:n + 1],
                     accum_out=SM[:, n:n + 1]).then_inc(s_p, 1)

            def pt_copy(n):
                h, qb = n // 4, n % 4
                act.wait_ge(s_pt, n + 1)
                if h >= 2:
                    act.wait_ge(s_pv, h - 1)
                act_(PT[h % 2][:, 0:qb + 1, qb * P:(qb + 1) * P],
                     bank[6 + qb % 2][:, 0:(qb + 1) * P].rearrange("p (a b) -> p a b", a=qb + 1),
                     ACT.Copy).then_inc(s_ptc, 1)

            def o_hi(h):
                act.wait_ge(s_pv, h + 1)
                act_(AH[:, h, :], bank[h % 2][:], ACT.Copy).then_inc(s_thi, 1)

            for n in range(4 * HEADS + 5):
                if n < 4 * HEADS:
                    exps(n)
                if n >= 3 and n - 3 < 4 * HEADS:
                    pt_copy(n - 3)
                if n >= 7 and n % 4 == 0:
                    o_hi((n - 8) // 4)
            def next_tile(name, key, kind, j, p, b):
                act.wait_ge(s_ev, b + 1)
                if kind != "final":
                    act_(one(GH, j), one(X, j), ACT.Identity, scale=gain(kind, j)).then_inc(s_thi, 1)
                square(one(X, j), SQ[p], key, j, p)

            def wo(i, last):
                for p in range(2):
                    b = FIRST["wo"] + 2 * i + p
                    act.wait_ge(s_mm, b + 1)
                    hi_next("wo", i, p, last)
                    next_tile("wo", "n_wo", "ffn0", 2 * i + p, p, b)
            pair_loop(act, 4, wo)

            def ffn(l, done):
                std(done[0])
                for t, (f0, n) in enumerate(THIRDS):
                    name = f"up{l}{t}"

                    def up(i, last):
                        for p in range(2):
                            b = FIRST[name] + 2 * i + p
                            c0 = 2 * NF * l + 2 * f0
                            act.wait_ge(s_mm, b + 1)
                            hi_next(name, i, p, last)
                            if p == 0 and not (isinstance(i, int) and i == 0):
                                gate(i - 1)
                            act.wait_ge(s_ev, b + 1)
                            w2 = CONV[:, c0 + 2 * i + p, 2:3] if isinstance(i, int) else \
                                CONV[:, bass.ds(c0 + 2 * i + p, 1), 2:3].rearrange("p a b -> p (a b)")
                            wb = CONV[:, c0 + 2 * i + p, 3:4] if isinstance(i, int) else \
                                CONV[:, bass.ds(c0 + 2 * i + p, 1), 3:4].rearrange("p a b -> p (a b)")
                            if p == 0 and not (isinstance(i, int) and i == 0):
                                act.wait_ge(s_h, NF * l + f0 + i)
                            act_(CV[p][:], Z[p][:, 2:S + 2], ACT.Identity, scale=w2, bias=wb).then_inc(s_c, 1)
                            if p == 0 and not (isinstance(i, int) and i == 0):
                                hid(i - 1)

                    def gate(i):
                        act.wait_ge(s_cv, NF * l + f0 + i + 1)
                        act_(SG[:], CV[1][:], ACT.Silu).then_inc(s_sg, 1)

                    def hid(i):
                        act.wait_ge(s_h, NF * l + f0 + i + 1)
                        act_(one(AH, i), HH[:], ACT.Copy).then_inc(s_thi, 1)
                    pair_loop(act, n, up)
                    gate(n - 1)
                    hid(n - 1)
                    dn = f"dn{l}{t}"

                    def down(i, last):
                        for p in range(2):
                            b = FIRST[dn] + 2 * i + p
                            act.wait_ge(s_mm, b + 1)
                            hi_next(dn, i, p, last)
                            if t == 2:
                                next_tile(dn, done[1], done[2], 2 * i + p, p, b)
                    pair_loop(act, KD // 2, down)

            ffn(0, ("n_wo", "n_dn02", "mix1"))

            std("n_dn02")

            def y_tile(j):
                act.wait_ge(s_yr, 128 * (j + 1))
                act_(one(AH, j).rearrange("p (k s) -> p s k", s=LQ), YB[:], ACT.Copy).then_inc(s_thi, 1)

            def gelu(j):
                act.wait_ge(s_Y, j + 1)
                if not (isinstance(j, int) and j == 0):
                    act.wait_ge(s_yw, 16 * j)
                for gi in range(2):
                    m = act_(Y2[:, gi::2, :], bank[6 + gi][:, 0:4 * NK].rearrange("p (a k) -> p a k", k=NK),
                             ACT.Gelu_apprx_tanh)
                m.then_inc(s_g, 1)

            def sort_lags(j, p):
                act.wait_ge(s_T, 16 * (j + 1))
                act_(TM[p][:].rearrange("p g s c -> p s g c"), TMR[:], ACT.Copy).then_inc(s_tm, 1)

            def s5_step(i, p):
                j = 2 * i + p
                if upto(j, 7):
                    act.wait_ge(s_mm, FIRST["win"] + j + 1)
                    hi("win", i + 1, p)
                if since(j, 1) and upto(j, 8):
                    sort_lags(j - 1, 1 - p)
                if since(j, 3):
                    y_tile(j - 3)
                if since(j, 2) and upto(j, 9):
                    gelu(j - 2)
            s5_loop(act, s5_step)

            def glu(i, last):
                for p in range(2):
                    b = FIRST["glu"] + 2 * i + p
                    act.wait_ge(s_mm, b + 1)
                    hi_next("glu", i, p, last)
                if not (isinstance(i, int) and i == 0):
                    act.wait_ge(s_ev, b - 1)
                act_(SIG[:], bank[1][:], ACT.Sigmoid).then_inc(s_sig, 1)
                next_tile("glu", "n_glu", "ffn1", i, 0, b)
            pair_loop(act, KD, glu)

            ffn(1, ("n_glu", "n_dn12", "final"))
            std("n_dn12")

        @block.vector
        def _(dve):
            v = nc.vector

            def lo(name, i, p):
                b = FIRST[name] + 2 * i + p
                n = UNITS[name] * P
                dve.wait_ge(s_hi, b + 1)
                v.tensor_tensor(WL[p][:, :n], RAW[p][:, :n], WH[p][:, :n].bitcast(F32), ALU.subtract).then_inc(s_lo, 1)

            def lo_next(name, i, p, last):
                if not last:
                    lo(name, i + 1, p)
                elif following(name):
                    lo(following(name), 0, p)

            def add_square(key, j, p, ss=None, first=False):
                ss = ss or SS
                n = SQ0[key] + j
                dve.wait_ge(s_sq, n + 1)
                if first:
                    v.tensor_copy(ss[:], SQ[p][:]).then_inc(s_ss, 1)
                else:
                    dve.wait_ge(s_ss, n)
                    v.tensor_tensor(ss[:], ss[:], SQ[p][:], ALU.add).then_inc(s_ss, 1)

            def rstd_cols(norm, col):
                dve.wait_ge(s_std, NORMS.index(norm) + 1)
                v.reciprocal(col[:], STD[:])
                v.drain()
                for t in range(TT):
                    m = v.tensor_scalar(DIAG[:, t, :], IDENT[:], col[:, t:t + 1], None, ALU.mult)
                m.then_inc(s_dg, 1)

            def rstd_copy(norm, dst):
                dve.wait_ge(s_bc, NORMS.index(norm) + 1)
                v.tensor_copy(dst[:], bank[3][:]).then_inc(s_rstd, 1)
                v.drain()

            def rstd(norm, dst, col):
                rstd_cols(norm, col)
                rstd_copy(norm, dst)

            v.memset(ONES[:], 1.0)
            v.memset(EPST[:], EPS).then_inc(s_const, 1)
            v.memset(KR[0][64:128, :], 0.0)
            v.memset(KR[1][0:64, :], 0.0)
            lo("wa", 0, 0)
            dve.wait_ge(s_par, 16 * 2)
            for k in range(KD):
                dve.wait_ge(s_thi, k + 1)
                v.scalar_tensor_tensor(out=GL[:, k, :], in0=X[:, k, :], scalar=gain("mix0", k),
                                       in1=GH[:, k, :].bitcast(F32), op0=ALU.mult, op1=ALU.subtract).then_inc(s_act, 1)
                add_square("x", k, k % 2, first=(k == 0))
                if k == 3:
                    lo("wa", 0, 1)
            rstd("x", RSTD, RCOL)

            def latent(b):
                v.tensor_tensor(CR[b % 2][:], bank[b % 2][:], RSTD[:], ALU.mult).then_inc(s_ev, 1)

            def latent_lo(b):
                g = gain("q", b) if b < KQ else gain("kv", b - KQ)
                dve.wait_ge(s_thi, TILE0["c"] + b + 1)
                v.scalar_tensor_tensor(out=AL[:, b, :], in0=CR[b % 2][:], scalar=g, in1=AH[:, b, :].bitcast(F32),
                                       op0=ALU.mult, op1=ALU.subtract).then_inc(s_act, 1)
                add_square("c", b, b % 2, ss=SS if b < KQ else SSKV, first=b in (0, KQ))

            def rotate(k, dst):
                dve.wait_ge(s_pm, k + 1)
                v.tensor_tensor(TMP[:], bank[6 + k % 2][:], SIN[:], ALU.mult).then_inc(s_rot, 1)
                v.tensor_tensor(RAWR[k % 4][:], RAWR[k % 4][:], COS[:], ALU.mult)
                v.drain()
                for rows, t in dst:
                    v.tensor_tensor(t, RAWR[k % 4][rows, :], TMP[rows, :], ALU.add)
                v.drain()

            for b in range(6):
                dve.wait_ge(s_mm, b + 1)
                lo_next("wa", b // 2, b % 2, b // 2 == 2)
                if b < 5:
                    latent(b)
                    latent_lo(b)
                if b == 3:
                    rstd_cols("q", RCOL)
                if b == 4:
                    rstd_copy("q", RSTDQ)
                if b == 5:
                    v.tensor_tensor(RAWR[0][:], bank[1][:], RSTD[:], ALU.mult).then_inc(s_ev, 1)
                    rstd_cols("kv", RCKV)

            dve.wait_ge(s_tab, 16 * 3)
            for b in range(6):
                gb = FIRST["uq"] + b
                dve.wait_ge(s_mm, gb + 1)
                lo_next("uq", b // 2, b % 2, b // 2 == 2)
                for u in range(2):
                    dst = RAWR[(2 * b + u + 1) % 4][:] if b < 2 else Qn[:, 2 * (b - 2) + u, :]
                    m = v.scalar_tensor_tensor(out=dst, in0=bank[b % 2 + 4 * u][:], scalar=SCALE, in1=RSTDQ[:],
                                               op0=ALU.mult, op1=ALU.mult)
                m.then_inc(s_ev, 1)
                if b == 0:
                    rstd_copy("kv", RSTDKV)
                    dve.wait_ge(s_trig, 4)
                    rotate(0, [(slice(0, 64), KR[0][0:64, :]), (slice(64, 128), KR[1][64:128, :])])
                if b == 3:
                    dve.wait_ge(s_ang, 6)
                    v.reciprocal(small["rden"][:], small["t3"][:]).then_inc(s_den, 1)
                if b in (1, 2):
                    for r in (2 * b - 2, 2 * b - 1):
                        rotate(r + 1, [(slice(0, 128), QR[:, r, :])])
            for b in range(2):
                dve.wait_ge(s_mm, FIRST["uk"] + b + 1)
                lo_next("uk", 0, b, True)
                for u, bk in enumerate(KV_BANKS[b]):
                    m = v.tensor_tensor(Kn[:, 4 * b + u, :], bank[bk][:], RSTDKV[:], ALU.mult)
                m.then_inc(s_ev, 1)
            for b in range(2):
                dve.wait_ge(s_mm, FIRST["uv"] + b + 1)
                if b == 0:
                    lo_next("uv", 0, b, True)
                for u, bk in enumerate(KV_BANKS[b]):
                    m = v.tensor_scalar(V[:, u, 512 * b:512 * b + 512], bank[bk][:], RCKV[:, u:u + 1], None, ALU.mult)
                m.then_inc(s_ev, 1)

            def row_max(n):
                qb = n % 4
                N = (qb + 1) * P
                dve.wait_ge(s_sc, n + 1)
                v.memset(bank[2 + qb][0:CHUNK, N - CHUNK:N], NEG)
                v.drain()
                v.tensor_reduce(MX[:, n:n + 1], bank[2 + qb][:, :N], AX.X, ALU.max, negate=True).then_inc(s_mx, 1)

            def normalize(n):
                qb = n % 4
                N = (qb + 1) * P
                dve.wait_ge(s_p, n + 1)
                v.reciprocal(RS[:, n:n + 1], SM[:, n:n + 1])
                v.drain()
                v.tensor_scalar(PR_[:, qb, :N], PR_[:, qb, :N], RS[:, n:n + 1], None, ALU.mult).then_inc(s_pn, 1)

            def o_lo(h):
                dve.wait_ge(s_thi, TILE0["o"] + h + 1)
                v.tensor_tensor(AL[:, h, :], bank[h % 2][:], AH[:, h, :].bitcast(F32), ALU.subtract).then_inc(s_act, 1)

            for n in range(4 * HEADS + 5):
                if n < 4 * HEADS:
                    row_max(n)
                if n == 1:
                    lo("wo", 0, 1)
                if 1 <= n <= 4 * HEADS:
                    normalize(n - 1)
                if n >= 7 and n % 4 == 0:
                    o_lo((n - 8) // 4)
            for p in range(2):
                v.memset(Z[p][:, 0:2], 0.0)
            v.drain()

            def next_tile(key, kind, j, p, first=False):
                if kind != "final":
                    dve.wait_ge(s_thi, TILE0[key] + j + 1)
                    v.scalar_tensor_tensor(out=one(GL, j), in0=one(X, j), scalar=gain(kind, j),
                                           in1=one(GH, j).bitcast(F32), op0=ALU.mult, op1=ALU.subtract).then_inc(s_act, 1)
                add_square(key, j, p, first=first)

            def add_x(b, j, p):
                v.tensor_tensor(one(X, j), bank[p][:], one(X, j), ALU.add).then_inc(s_ev, 1)

            def wo(i, last):
                for p in range(2):
                    b = FIRST["wo"] + 2 * i + p
                    dve.wait_ge(s_mm, b + 1)
                    lo_next("wo", i, p, last)
                    add_x(b, 2 * i + p, p)
                    next_tile("n_wo", "ffn0", 2 * i + p, p, first=isinstance(i, int) and i == 0 and p == 0)
            pair_loop(dve, 4, wo)

            def ffn(l, done):
                rstd(done[0], RSTD, RCOL)
                for t, (f0, n) in enumerate(THIRDS):
                    name = f"up{l}{t}"
                    hk = f"h{l}{t}"
                    c0 = 2 * NF * l + 2 * f0

                    def tap(k, i, p):
                        if isinstance(i, int):
                            return CONV[:, c0 + 2 * i + p, k:k + 1]
                        return CONV[:, bass.ds(c0 + 2 * i + p, 1), k:k + 1].rearrange("p a b -> p (a b)")

                    def hidden(i):
                        dve.wait_ge(s_sg, NF * l + f0 + i + 1)
                        v.tensor_tensor(HH[:], SG[:], CV[0][:], ALU.mult).then_inc(s_h, 1)

                    def hidden_lo(i):
                        dve.wait_ge(s_thi, TILE0[hk] + i + 1)
                        v.tensor_tensor(one(AL, i), HH[:], one(AH, i).bitcast(F32), ALU.subtract).then_inc(s_act, 1)

                    def up(i, last):
                        first = isinstance(i, int) and i == 0
                        for p in range(2):
                            b = FIRST[name] + 2 * i + p
                            dve.wait_ge(s_mm, b + 1)
                            if not (last and p == 1):
                                lo_next(name, i, p, last)
                            v.tensor_tensor(Z[p][:, 2:S + 2], bank[p][:], RSTD[:], ALU.mult).then_inc(s_ev, 1)
                            if last and p == 1:
                                lo_next(name, i, p, last)
                            if p == 0 and not first:
                                hidden(i - 1)
                            dve.wait_ge(s_c, 2 * (NF * l + f0 + i) + p + 1)
                            v.scalar_tensor_tensor(out=CV[p][:], in0=Z[p][:, 1:S + 1], scalar=tap(1, i, p),
                                                   in1=CV[p][:], op0=ALU.mult, op1=ALU.add)
                            v.drain()
                            m = v.scalar_tensor_tensor(out=CV[p][:], in0=Z[p][:, 0:S], scalar=tap(0, i, p),
                                                       in1=CV[p][:], op0=ALU.mult, op1=ALU.add)
                            if p == 0 and not first:
                                hidden_lo(i - 1)
                        m.then_inc(s_cv, 1)
                    pair_loop(dve, n, up)
                    hidden(n - 1)
                    hidden_lo(n - 1)
                    dn = f"dn{l}{t}"

                    def down(i, last):
                        for p in range(2):
                            b = FIRST[dn] + 2 * i + p
                            dve.wait_ge(s_mm, b + 1)
                            lo_next(dn, i, p, last)
                            add_x(b, 2 * i + p, p)
                            if t == 2:
                                next_tile(done[1], done[2], 2 * i + p, p, first=isinstance(i, int) and i == 0 and p == 0)
                    pair_loop(dve, KD // 2, down)

            ffn(0, ("n_wo", "n_dn02", "mix1"))

            v.memset(ZERO[:], 0.0).then_inc(s_zz, 1)
            rstd("n_dn02", RSTD, RCOL)
            dve.wait_ge(s_kz, 128)
            for p in range(2):
                v.memset(XR[p][:, :, 0:1], 0.0)
                v.memset(XI[p][:, :, 0:1], 0.0)

            def u_out(j, p):
                if not (isinstance(j, int) and j == 0):
                    dve.wait_ge(s_uw, 16 * j)
                v.tensor_tensor(UB[:], bank[p][:].rearrange("p (k s) -> p s k", s=LQ),
                                RSTD[:].rearrange("p (k s) -> p s k", s=LQ), ALU.mult).then_inc(s_ev, 1)

            def matrices(j, p):
                dve.wait_ge(s_et, j + 1)
                if not (isinstance(j, int) and j < 2):
                    dve.wait_ge(s_E, j - 1)
                    dve.wait_ge(s_kw, 16 * (j - 1))
                for r in range(2):
                    v.tensor_copy(ET[p][:, r, :, :], bank[4 + r][:].rearrange("p (q m) -> p q m", q=4))
                dc = DCOL[:, 8 * j:8 * j + 8] if isinstance(j, int) else DCOL[:, bass.ds(8 * j, 8)]
                v.tensor_tensor(KALL[p][:], MASK[:].unsqueeze(1).broadcast_to([P, 8, C]),
                                dc.unsqueeze(2).broadcast_to([P, 8, C]), ALU.mult)
                v.drain()
                v.tensor_tensor(KALL[p][:], KALL[p][:], bank[3][:, 0:P].rearrange("p (g c) -> p g c", c=C),
                                ALU.add).then_inc(s_kall, 1)

            def cols(t, j):
                return t[:, 4 * j:4 * j + 4, :].rearrange("p q k -> p (q k)") if isinstance(j, int) else \
                    t[:, bass.ds(4 * j, 4), :].rearrange("p q k -> p (q k)")

            def states(j, p):
                n = 4 * NK
                dve.wait_ge(s_E, j + 1)
                er, ei = bank[2][:, 0:n], bank[2][:, n:2 * n]
                a, b_, c_, e, a2, c2 = (t[:] for t in R4)
                v.tensor_tensor(a, er, cols(WC, j), ALU.mult)
                v.tensor_tensor(b_, ei, cols(WS, j), ALU.mult)
                v.tensor_tensor(c_, ei, cols(WC, j), ALU.mult)
                v.tensor_tensor(e, er, cols(WS, j), ALU.mult)
                v.drain()
                v.tensor_tensor(a, a, b_, ALU.add)
                v.tensor_tensor(c_, c_, e, ALU.subtract)
                v.drain()
                v.tensor_tensor_scan(b_, cols(RT, j), a, 0.0, ALU.mult, ALU.add)
                v.tensor_tensor_scan(e, cols(RT, j), c_, 0.0, ALU.mult, ALU.add)
                v.drain()
                q = "p (q k) -> p q k"
                wc, ws = cols(WC, j).rearrange(q, k=NK), cols(WS, j).rearrange(q, k=NK)
                zr, zi = b_.rearrange(q, k=NK), e.rearrange(q, k=NK)
                t1, t2, t3, t4 = (t.rearrange(q, k=NK) for t in (a, c_, a2, c2))
                v.tensor_tensor(t1, zr, wc, ALU.mult)
                v.tensor_tensor(t2, zi, ws, ALU.mult)
                v.tensor_tensor(t3, zr, ws, ALU.mult)
                v.tensor_tensor(t4, zi, wc, ALU.mult)
                v.drain()
                v.tensor_tensor(XR[p][:, :, 1:], t1, t2, ALU.subtract)
                v.tensor_tensor(XI[p][:, :, 1:], t3, t4, ALU.add).then_inc(s_X, 1)

            def y_lo(j):
                dve.wait_ge(s_thi, TILE0["y"] + j + 1)
                t = "p (k s) -> p s k"
                v.tensor_tensor(one(AL, j).rearrange(t, s=LQ), YB[:], one(AH, j).bitcast(F32).rearrange(t, s=LQ),
                                ALU.subtract).then_inc(s_act, 1)

            def s5_step(i, p):
                j = 2 * i + p
                if upto(j, 7):
                    dve.wait_ge(s_mm, FIRST["win"] + j + 1)
                    u_out(j, p)
                    lo("win", i + 1, p)
                if isinstance(j, int) and j == 1:
                    states(0, 0)
                if since(j, 3):
                    y_lo(j - 3)
                if upto(j, 7):
                    matrices(j, p)
                if since(j, 2) and upto(j, 8):
                    states(j - 1, 1 - p)
            s5_loop(dve, s5_step)

            def glu(i, last):
                first = isinstance(i, int) and i == 0
                for p in range(2):
                    b = FIRST["glu"] + 2 * i + p
                    dve.wait_ge(s_mm, b + 1)
                    lo_next("glu", i, p, last)
                    if p == 0:
                        v.tensor_copy(VAL[:], bank[0][:]).then_inc(s_ev, 1)
                v.drain()
                dve.wait_ge(s_sig, i + 1)
                v.tensor_tensor(VAL[:], VAL[:], SIG[:], ALU.mult)
                v.drain()
                v.tensor_tensor(one(X, i), VAL[:], one(X, i), ALU.add).then_inc(s_ev, 1)
                next_tile("n_glu", "ffn1", i, 0, first=first)
            pair_loop(dve, KD, glu)
            for p in range(2):
                v.memset(Z[p][:, 0:2], 0.0)
            v.drain()
            ffn(1, ("n_glu", "n_dn12", "final"))
            rstd("n_dn12", RSTD, RCOL)
            for k in range(KD):
                v.scalar_tensor_tensor(out=X[:, k, :], in0=X[:, k, :], scalar=gain("final", k), in1=RSTD[:],
                                       op0=ALU.mult, op1=ALU.mult).then_inc(s_fin, 1)

        @block.gpsimd
        def _(pool):
            g = nc.gpsimd
            sm = small

            def tt(out, a, b, op):
                return g.tensor_tensor(out, a, b, op)

            def cmul(o_r, o_i, ar, ai, br, bi, t1, t2, done=None):
                tt(t1, ar, br, ALU.mult)
                tt(t2, ai, bi, ALU.mult)
                g.drain()
                tt(o_r, t1, t2, ALU.subtract)
                g.drain()
                tt(t1, ar, bi, ALU.mult)
                tt(t2, ai, br, ALU.mult)
                g.drain()
                m = tt(o_i, t1, t2, ALU.add)
                if done is not None:
                    m.then_inc(done, 1)
                g.drain()

            f = {n: t[:] for n, t in small.items()}

            def reduce_angle(dst, ang, k, t, cosine):
                g.tensor_scalar(k, ang, 1.0 / TWO_PI, 0.25 if cosine else 0.0, ALU.mult, ALU.add)
                g.drain()
                g.tensor_scalar(k, k, MAGIC, MAGIC, ALU.add, ALU.subtract)
                g.drain()
                src = ang
                for part in (PI_1, PI_2, PI_3):
                    g.tensor_scalar(t, k, -part, None, ALU.mult)
                    g.drain()
                    tt(dst, src, t, ALU.add)
                    g.drain()
                    src = dst
                if cosine:
                    g.tensor_scalar(dst, dst, np.pi / 2, None, ALU.add)
                    g.drain()
                g.tensor_scalar(dst, dst, PI_IN, -PI_IN, ALU.min, ALU.max).then_inc(s_ang, 1)

            pool.wait_ge(s_pos, 16 * 5)
            pool.wait_ge(s_trig, 1)
            tt(f["ldt"], f["lr"], f["dt"], ALU.mult).then_inc(s_ang, 1)
            tt(f["th"], f["li"], f["dt"], ALU.mult)
            g.tensor_copy(POSF[:], POSI[:])
            g.drain()
            g.tensor_scalar(POSF[:], POSF[:], INV[:, 0:1], None, ALU.mult)
            g.drain()
            reduce_angle(COS[:], POSF[:], KANG[:], KTMP[:], True)
            reduce_angle(SIN[:], POSF[:], KANG[:], KTMP[:], False)
            g.drain()
            reduce_angle(f["cs"], f["th"], f["k"], f["t1"], True)
            reduce_angle(f["sn"], f["th"], f["k"], f["t1"], False)
            g.drain()
            tt(f["t1"], f["lr"], f["lr"], ALU.mult)
            tt(f["t2"], f["li"], f["li"], ALU.mult)
            g.drain()
            tt(f["t3"], f["t1"], f["t2"], ALU.add).then_inc(s_ang, 1)
            pool.wait_ge(s_trig, 6)
            pool.wait_ge(s_den, 1)
            tt(f["ar"], f["mag"], f["cs"], ALU.mult)
            tt(f["ai"], f["mag"], f["sn"], ALU.mult)
            g.drain()
            g.tensor_scalar(f["r"], f["ar"], -1.0, None, ALU.add)
            g.drain()
            tt(f["t1"], f["r"], f["lr"], ALU.mult)
            tt(f["t2"], f["ai"], f["li"], ALU.mult)
            g.drain()
            tt(f["t1"], f["t1"], f["t2"], ALU.add)
            g.drain()
            tt(f["cr"], f["t1"], f["rden"], ALU.mult)
            g.drain()
            tt(f["t1"], f["ai"], f["lr"], ALU.mult)
            tt(f["t2"], f["r"], f["li"], ALU.mult)
            g.drain()
            tt(f["t1"], f["t1"], f["t2"], ALU.subtract)
            g.drain()
            tt(f["ci"], f["t1"], f["rden"], ALU.mult)
            tt(f["r8"], f["mag"], f["mag"], ALU.mult)
            g.drain()
            for _ in range(2):
                tt(f["t1"], f["r8"], f["r8"], ALU.mult)
                g.drain()
                g.tensor_copy(f["r8"], f["t1"])
                g.drain()
            cmul(f["wr"], f["wi"], f["cs"], f["sn"], f["cs"], f["sn"], f["t1"], f["t2"])
            cmul(f["k"], f["th"], f["wr"], f["wi"], f["wr"], f["wi"], f["t1"], f["t2"])
            cmul(f["wr"], f["wi"], f["k"], f["th"], f["k"], f["th"], f["t1"], f["t2"])

            pool.wait_ge(s_mm, FIRST["wo"] + BLOCKS["wo"])
            g.memset(PWR[:, 0, :], 1.0)
            g.memset(PWI[:, 0, :], 0.0)
            g.drain()
            for k in range(LQ):
                cmul(PWR[:, k + 1, :], PWI[:, k + 1, :], PWR[:, k, :], PWI[:, k, :], f["ar"], f["ai"], f["t1"], f["t2"])
            g.memset(WC[:, :, 0:1], 1.0)
            g.memset(WS[:, :, 0:1], 0.0)
            g.drain()
            n = 1
            wk = ((f["wr"], f["wi"]), (f["k"], f["th"]))
            t1, t2 = PT1_[:], PT2_[:]
            while n < NK:
                (wr, wi), other = wk
                half = max(1, NQ * n // 512)
                nq = NQ // half
                for q0 in range(0, NQ, nq):
                    def bc(x):
                        return x[:, q0:q0 + nq].unsqueeze(2).broadcast_to([P, nq, n])

                    def tmp(t):
                        return t[:, 0:nq * n].rearrange("p (q k) -> p q k", k=n)
                    sl = slice(q0, q0 + nq)
                    cmul(WC[:, sl, n:2 * n], WS[:, sl, n:2 * n], WC[:, sl, 0:n], WS[:, sl, 0:n], bc(wr), bc(wi),
                         tmp(t1), tmp(t2))
                n *= 2
                if n < NK:
                    cmul(other[0], other[1], wr, wi, wr, wi, f["t1"], f["t2"])
                    wk = (other, (wr, wi))
            g.tensor_copy(RT[:], f["r8"].unsqueeze(2).broadcast_to([P, NQ, NK]))
            g.drain()
            g.memset(RT[:, :, 0:1], 0.0)
            pool.wait_ge(s_spar, 16 * 7)
            big = PT1_[:, 0:NQ * C].rearrange("p (q c) -> p q c", c=C)
            big2 = PT2_[:, 0:NQ * C].rearrange("p (q c) -> p q c", c=C)
            cmul(BBR[:], BBI[:], f["cr"].unsqueeze(2).broadcast_to([P, NQ, C]),
                 f["ci"].unsqueeze(2).broadcast_to([P, NQ, C]), BRE[:], BIM[:], big, big2)
            g.tensor_scalar(CIN[:], CIN[:], -1.0, None, ALU.mult)
            g.tensor_scalar(CBI[:], CBI[:], -1.0, None, ALU.mult)
            g.drain()

            def views(j):
                sh = [P, 4, LQ, C]

                def pw(t, m0):
                    x = t[:, m0:m0 + LQ, 4 * j:4 * j + 4] if isinstance(j, int) else t[:, m0:m0 + LQ, bass.ds(4 * j, 4)]
                    return x.rearrange("p m q -> p q m").unsqueeze(3).broadcast_to(sh)

                def ch(t):
                    x = t[:, 4 * j:4 * j + 4, :] if isinstance(j, int) else t[:, bass.ds(4 * j, 4), :]
                    return x.unsqueeze(2).broadcast_to(sh)
                a = PT1_[:].rearrange("p (q m c) -> p q m c", q=4, m=LQ)
                b_ = PT2_[:].rearrange("p (q m c) -> p q m c", q=4, m=LQ)
                return pw, ch, a, b_

            def outputs(j, p):
                pw, ch, a, b_ = views(j)
                if not (isinstance(j, int) and j < 2):
                    pool.wait_ge(s_ow[p], 8 * (j - p))
                tt(a, pw(PWR, 1), ch(CRE), ALU.mult)
                tt(b_, pw(PWI, 1), ch(CIN), ALU.mult)
                g.drain()
                tt(OR[p], a, b_, ALU.add)
                g.drain()
                tt(a, pw(PWR, 1), ch(CIN), ALU.mult)
                tt(b_, pw(PWI, 1), ch(CRE), ALU.mult)
                g.drain()
                tt(OI[p], a, b_, ALU.subtract).then_inc(s_O, 1)
                pool.wait_ge(s_O, j + 1)
                g.dma_start(OD[j] if isinstance(j, int) else OD[bass.ds(j, 1)].rearrange("a p r n -> (a p) r n"),
                            OO[p][:]).then_inc(s_ow[p], 16)

            def inputs(j):
                pw, ch, a, b_ = views(j)
                if not (isinstance(j, int) and j == 0):
                    pool.wait_ge(s_et, j)
                cmul(GR[:], GI[:], pw(PWR, 0), pw(PWI, 0), ch(BBR), ch(BBI), a, b_, s_G)

            for j in range(2):
                outputs(j, j)
            with pool.Fori(1, 4) as i:
                for p in range(2):
                    outputs(2 * i + p, p)
            for p in range(2):
                pool.wait_ge(s_ow[p], 16 * 4)
            inputs(0)
            with pool.Fori(1, 8) as j:
                inputs(j)

        @block.tensor
        def _(pe):
            mm = nc.tensor.matmul

            def unit(out, w, u, hi_, lo_, k, start, stop):
                wh, wl = WH[w][:, u * P:(u + 1) * P], WL[w][:, u * P:(u + 1) * P]
                mm(out, wh, hi_[:, k, :], start=start, stop=False)
                mm(out, wh, lo_[:, k, :], start=False, stop=False)
                return mm(out, wl, hi_[:, k, :], start=False, stop=stop)

            def ready(b):
                pe.wait_ge(s_lo, b + 1)
                if not (isinstance(b, int) and b < 2):
                    pe.wait_ge(s_ev, b - 1)

            def stats(norm, ss=None):
                ss = ss or SS
                pe.wait_ge(s_ss, SQ_END[norm])
                for t in range(TT):
                    m = mm(bank[2][:, t:t + 1], ss[:, t * P:(t + 1) * P], ONES[:, 0:1], start=True, stop=True)
                m.then_inc(s_st, 1)

            def bcast(norm):
                pe.wait_ge(s_dg, NORMS.index(norm) + 1)
                mm(bank[3][:], ONES[:], DIAG[:].rearrange("p a b -> p (a b)"), start=True, stop=True).then_inc(s_bc, 1)

            def first_pair(name, tile0, n, hi_, lo_, norm=None, ahead=0, ss=None):
                B = FIRST[name]
                ready(B)
                if name == "wo":
                    pe.wait_ge(s_act, tile0 + HEADS - 1)
                for k in range(n - 1):
                    if name != "wo":
                        pe.wait_ge(s_act, tile0 + k + 1)
                    unit(bank[0][:], 0, k, hi_, lo_, k, k == 0, False)

                def second(k):
                    if k == 0:
                        ready(B + 1)
                    unit(bank[1][:], 1, k, hi_, lo_, k, k == 0, k == n - 1)
                for k in range(ahead):
                    second(k)
                pe.wait_ge(s_act, tile0 + n)
                unit(bank[0][:], 0, n - 1, hi_, lo_, n - 1, False, True).then_inc(s_mm, 1)
                if norm:
                    stats(norm)
                for k in range(ahead, n - 1):
                    if norm and k == n - 2:
                        bcast(norm)
                    second(k)
                unit(bank[1][:], 1, n - 1, hi_, lo_, n - 1, False, True).then_inc(s_mm, 1)

            def other_pairs(name, n, hi_, lo_):
                def pair(i):
                    for p in range(2):
                        ready(FIRST[name] + 2 * i + p)
                        for k in range(n):
                            m = unit(bank[p][:], p, k, hi_, lo_, k, k == 0, k == n - 1)
                        m.then_inc(s_mm, 1)
                if BLOCKS[name] == 4:
                    pair(1)
                else:
                    with pe.Fori(1, BLOCKS[name] // 2) as i:
                        pair(i)

            pe.wait_ge(s_const, 1)
            first_pair("wa", TILE0["x"], KD, GH, GL, norm="x")
            for b in range(2, 6):
                ready(b)
                for k in range(KD):
                    m = unit(bank[b % 2][:], b % 2, k, GH, GL, k, k == 0, k == KD - 1)
                m.then_inc(s_mm, 1)
                if b == 3:
                    stats("q")
                if b == 4:
                    bcast("q")
            stats("kv", SSKV)

            def permute(k):
                if k >= 2:
                    pe.wait_ge(s_rot, k - 1)
                mm(bank[6 + k % 2][:], PERM[:], RAWR[k % 4][:], start=True, stop=True).then_inc(s_pm, 1)
            for b in range(6):
                B = FIRST["uq"] + b
                ready(B)
                if b == 0:
                    pe.wait_ge(s_act, TILE0["c"] + KQ)
                for u in range(2):
                    for k in range(KQ):
                        m = unit(bank[b % 2 + 4 * u][:], b % 2, KQ * u + k, AH, AL, k, k == 0, k == KQ - 1)
                m.then_inc(s_mm, 1)
                if b == 0:
                    bcast("kv")
                    pe.wait_ge(s_tab, 16 * 3)
                    pe.wait_ge(s_ev, 6)
                    permute(0)
                if b in (1, 2):
                    pe.wait_ge(s_ev, B)
                    permute(2 * b - 1)
                    permute(2 * b)
            for b in range(2):
                ready(FIRST["uk"] + b)
                if b == 0:
                    pe.wait_ge(s_act, TILE0["c"] + KQ + KKV)
                    pe.wait_ge(s_rot, 5)
                for u, bk in enumerate(KV_BANKS[b]):
                    for k in range(KKV):
                        m = unit(bank[bk][:], b, KKV * u + k, AH, AL, KQ + k, k == 0, k == KKV - 1)
                m.then_inc(s_mm, 1)
            for b in range(2):
                ready(FIRST["uv"] + b)
                for u, bk in enumerate(KV_BANKS[b]):
                    for k in range(KKV):
                        ts = slice(u * P, (u + 1) * P)
                        wh, wl = WH[b][:, 512 * k:512 * k + 512], WL[b][:, 512 * k:512 * k + 512]
                        mm(bank[bk][:], AH[:, KQ + k, ts], wh, start=(k == 0), stop=False)
                        mm(bank[bk][:], AH[:, KQ + k, ts], wl, start=False, stop=False)
                        m = mm(bank[bk][:], AL[:, KQ + k, ts], wh, start=False, stop=(k == KKV - 1))
                m.then_inc(s_mm, 1)

            def scores(n):
                h, qb = n // 4, n % 4
                N = (qb + 1) * P
                if n >= 4:
                    pe.wait_ge(s_p, n - 3)
                qs = slice(qb * P, (qb + 1) * P)
                mm(bank[2 + qb][:, :N], Qn[:, h, qs], Kn[:, h, :N], start=True, stop=False)
                mm(bank[2 + qb][:, :N], QR[:, h // 2, qs], KR[h % 2][:, :N], start=False, stop=True).then_inc(s_sc, 1)

            def turn(n):
                qb = n % 4
                pe.wait_ge(s_pn, n + 1)
                if n >= 2:
                    pe.wait_ge(s_ptc, n - 1)
                for kb in range(qb + 1):
                    m = nc.tensor.transpose(bank[6 + qb % 2][:, kb * P:(kb + 1) * P],
                                            PR_[:, qb, kb * P:(kb + 1) * P], IDENT[:])
                m.then_inc(s_pt, 1)

            def pv(h):
                pe.wait_ge(s_ptc, 4 * h + 4)
                if h >= 2:
                    pe.wait_ge(s_act, TILE0["o"] + h - 1)
                for kb in range(TT):
                    m = mm(bank[h % 2][:, kb * P:], V[:, kb, h * VH:(h + 1) * VH], PT[h % 2][:, kb, kb * P:],
                           start=(kb == 0), stop=(kb == TT - 1))
                m.then_inc(s_pv, 1)

            pe.wait_ge(s_ev, FIRST["uv"] + 1)
            for n in range(4 * HEADS + 4):
                if n == 1:
                    pe.wait_ge(s_ev, FIRST["wo"])
                if n < 4 * HEADS:
                    scores(n)
                if 3 <= n < 4 * HEADS + 3:
                    turn(n - 3)
                if n >= 7 and n % 4 == 3:
                    pv((n - 7) // 4)
            first_pair("wo", TILE0["o"], HEADS, AH, AL)
            other_pairs("wo", KD, AH, AL)

            def ffn(l, norm, tile0):
                for t, (f0, n) in enumerate(THIRDS):
                    first_pair(f"up{l}{t}", tile0, KD, GH, GL, norm=norm if t == 0 else None)
                    other_pairs(f"up{l}{t}", KD, GH, GL)
                    first_pair(f"dn{l}{t}", TILE0[f"h{l}{t}"], n, AH, AL, ahead=n // 2)
                    other_pairs(f"dn{l}{t}", n, AH, AL)
            ffn(0, "n_wo", TILE0["n_wo"])

            def matrices(j, p):
                pe.wait_ge(s_G, j + 1)
                if isinstance(j, int) and j == 0:
                    pe.wait_ge(s_rstd, NORMS.index("n_dn02") + 1)
                if not (isinstance(j, int) and j == 0):
                    pe.wait_ge(s_kall, j)
                for r, src in enumerate((GR, GI)):
                    for q in range(4):
                        nc.tensor.transpose(bank[4 + r][:, q * P:(q + 1) * P],
                                            src[:, q, :, :].rearrange("p m c -> p (m c)"), IDENT[:])
                for q in range(4):
                    cs = slice(q * 2 * C, (q + 1) * 2 * C)
                    c = [t[:, 4 * j + q, :] if isinstance(j, int) else
                         t[:, bass.ds(4 * j + q, 1), :].rearrange("p a c -> p (a c)") for t in (CBR, CBI)]
                    mm(bank[3][:, cs], GR[:, q, :, :].rearrange("p m c -> p (m c)"), c[0], start=True, stop=False)
                    m = mm(bank[3][:, cs], GI[:, q, :, :].rearrange("p m c -> p (m c)"), c[1], start=False, stop=True)
                m.then_inc(s_et, 1)

            def outputs(i, p):
                j = 2 * i + p
                pe.wait_ge(s_X, j - 1)
                pe.wait_ge(s_tm, j - 1)
                pe.wait_ge(s_or[p], 16 * i)
                if not (isinstance(j, int) and j == 2):
                    pe.wait_ge(s_g, j - 2)
                for q in range(4):
                    for gi in range(2):
                        rows = slice(64 * gi, 64 * gi + 64)
                        gg = 2 * q + gi
                        out = bank[6 + gi][:, q * NK:(q + 1) * NK]
                        mm(out, TM[p][:, gg, :, :].rearrange("p s c -> p (s c)"), U2[p][:, gg, :],
                           start=True, stop=False)
                        mm(out, OR[p][rows, q, :, :].rearrange("p m c -> p (m c)"), XR[p][rows, q, 0:NK],
                           start=False, stop=False)
                        m = mm(out, OI[p][rows, q, :, :].rearrange("p m c -> p (m c)"), XI[p][rows, q, 0:NK],
                               start=False, stop=True)
                m.then_inc(s_Y, 1)

            def chunk_inputs(i, p):
                j = 2 * i + p
                w = 1 - p
                pe.wait_ge(s_ur[w], 128 * (i + p))
                pe.wait_ge(s_kall, j)
                if not (isinstance(j, int) and j == 1):
                    pe.wait_ge(s_X, j - 1)
                for q in range(4):
                    for r in range(2):
                        for gi in range(2):
                            rows = slice(64 * gi, 64 * gi + 64)
                            c0 = (4 * r + q) * NK
                            m = mm(bank[2][rows, c0:c0 + NK], ET[w][:, r, q, rows], U2[w][:, 2 * q + gi, :],
                                   start=True, stop=True)
                m.then_inc(s_E, 1)

            def tokens(j, p):
                ready(FIRST["win"] + j)
                for k in range(KD):
                    m = unit(bank[p][:], p, k, GH, GL, k, k == 0, k == KD - 1)
                m.then_inc(s_mm, 1)

            def s5_step(i, p):
                j = 2 * i + p
                if isinstance(j, int) and j == 1:
                    return
                if isinstance(j, int) and j == 2:
                    tokens(2, 0)
                    chunk_inputs(0, 1)
                    matrices(1, 1)
                if since(j, 2) and upto(j, 6):
                    tokens(j + 1, 1 - p)
                if isinstance(j, int) and j == 7:
                    glu_steps(range(0, 4), [0])
                if isinstance(j, int) and j == 8:
                    glu_steps(range(0, 4), [1])
                    chunk_inputs(i, p)
                if since(j, 2) and upto(j, 9):
                    outputs(i, p)
                if upto(j, 7):
                    matrices(j, p)
                if since(j, 1) and upto(j, 7):
                    chunk_inputs(i, p)

            def glu_steps(ks, blocks=(0, 1)):
                for p in blocks:
                    for k in ks:
                        if k == 0:
                            ready(FIRST["glu"] + p)
                        pe.wait_ge(s_act, TILE0["y"] + k + 1)
                        m = unit(bank[p][:], p, k, AH, AL, k, k == 0, k == KD - 1)
                    if KD - 1 in ks:
                        m.then_inc(s_mm, 1)

            first_pair("win", TILE0["n_dn02"], KD, GH, GL, norm="n_dn02")
            for j in range(3):
                s5_step(j // 2, j % 2)
            with pe.Fori(1, 3) as i:
                s5_step(i, 1)
                s5_step(i + 1, 0)
            for j in range(7, 11):
                s5_step(j // 2, j % 2)
            glu_steps(range(4, KD - 1))
            glu_steps([KD - 1])
            other_pairs("glu", KD, AH, AL)
            ffn(1, "n_glu", TILE0["n_glu"])
            stats("n_dn12")
            bcast("n_dn12")


KV_BANKS = ((0, 4, 6, 2), (1, 5, 7, 3))


def kernel(**inp):
    import concourse.bacc as bacc
    from concourse.bass_utils import run_bass_kernel_spmd as run

    a = {k: np.asarray(v) for k, v in inp.items()}
    arrays = {}

    def put(name, x):
        arrays[name] = np.ascontiguousarray(x)

    def blocks(w, n=P):
        k, m = w.shape
        return w.reshape(k // P, P, m // n, n).transpose(2, 1, 0, 3).reshape(m // n, P, k // P * n)

    def halves(x):
        x = x.reshape((NQ, 2, PS) + x.shape[2:])
        return np.moveaxis(x, 0, 2).reshape((2 * PS, NQ) + x.shape[3:])

    put("x", a["x"][0].T.reshape(KD, P, S))
    put("pos", a["positions"][0])
    put("inv", np.tile((1.0 / (np.float32(THETA) ** (np.arange(0, ROPE, 2, dtype=np.float32) / np.float32(ROPE)))
                        ).astype(np.float32), 4)[:, None])
    cols = lambda g: g.reshape(-1, P).T
    put("gain", np.concatenate([cols(a["g_mix"][0]), cols(a["g_mix"][1]), cols(a["g_ffn"][0]), cols(a["g_ffn"][1]),
                                cols(a["g_final"]), cols(a["mla_g_q"][0]), cols(a["mla_g_kv"][0])], axis=1))
    put("ident", np.eye(P, dtype=np.float32))
    perm = np.zeros((P, P), np.float32)
    for r in range(P):
        o = r % 64
        perm[r + 32 if o < 32 else r - 32, r] = -1.0 if o < 32 else 1.0
    put("perm", perm)
    cw = np.concatenate([a["ffn_conv_w"], a["ffn_conv_b"][:, None, :]], axis=1)
    put("conv", cw.reshape(DEPTH, 4, 2, NF, P).transpose(4, 0, 3, 2, 1).reshape(P, DEPTH * 2 * NF, 4))

    wa = a["mla_w_a"][0]
    kr = wa[:, Q_LORA + KV_LORA:]
    put("w_wa", blocks(np.concatenate([wa[:, :Q_LORA + KV_LORA], kr, kr], axis=1)))
    uq = a["mla_w_uq"][0].reshape(Q_LORA, HEADS, NOPE + ROPE)
    uq = np.concatenate([uq[:, :, NOPE:].reshape(Q_LORA, HEADS * ROPE), uq[:, :, :NOPE].reshape(Q_LORA, HEADS * NOPE)], 1)
    put("w_uq", blocks(uq).reshape(6, 2, P, KQ * P).transpose(0, 2, 1, 3).reshape(6, P, 2 * KQ * P))
    ukv = a["mla_w_ukv"][0].reshape(KV_LORA, HEADS, NOPE + VH)
    put("w_uk", blocks(ukv[:, :, :NOPE].reshape(KV_LORA, HEADS * NOPE)).reshape(2, 4, P, KKV * P)
        .transpose(0, 2, 1, 3).reshape(2, P, 8 * P))
    put("w_uv", blocks(ukv[:, :, NOPE:].reshape(KV_LORA, HEADS * VH), 512))
    put("w_wo", blocks(a["mla_w_o"][0]))
    put("w_win", blocks(a["ssm_w_in"][0]))
    glu = a["ssm_w_glu"][0].reshape(D, 2, KD, P).transpose(0, 2, 1, 3).reshape(D, 2 * D)
    put("w_glu", blocks(glu))
    for l in range(DEPTH):
        up = a["ffn_w_up"][l].reshape(D, 2, NF, P).transpose(0, 2, 1, 3)
        for t, (f0, n) in enumerate(THIRDS):
            put(f"w_up{l}{t}", blocks(up[:, f0:f0 + n].reshape(D, 2 * n * P)))
            put(f"w_dn{l}{t}", blocks(a["ffn_w_down"][l][f0 * P:(f0 + n) * P]))

    put("lr", halves(a["ssm_lambda_re"][0]))
    put("li", halves(a["ssm_lambda_im"][0]))
    put("ld", halves(np.broadcast_to(a["ssm_log_dt"][0][:, None], (G, PS))))
    put("bre", halves(a["ssm_b_re"][0]))
    put("bim", halves(a["ssm_b_im"][0]))
    for n, src in (("re", "ssm_c_re"), ("im", "ssm_c_im")):
        c = halves(a[src][0].transpose(0, 2, 1))
        put("c" + n, c)
        bd = np.zeros((P, NQ, 2 * C), np.float32)
        bd[:PS, :, :C] = c[:PS]
        bd[PS:, :, C:] = c[PS:]
        put("cb" + n[0], bd)
    dcol = np.zeros((P, G), np.float32)
    dcol[:C] = a["ssm_d"][0].reshape(G, C).T
    put("dcol", dcol)
    mask = np.zeros((P, C), np.float32)
    mask[:C] = np.eye(C, dtype=np.float32)
    put("mask", mask)

    nc = bacc.Bacc("TRN2", target_bir_lowering=False, num_devices=1, dynamic_dma_scratch_size=1024)
    d = {}
    for name, x in arrays.items():
        d[name] = nc.dram_tensor("in_" + name, x.shape, mybir.dt.from_np(x.dtype), kind="ExternalInput").ap()
    d["out"] = nc.dram_tensor("out", (KD, P, S), F32, kind="ExternalOutput").ap()
    build(nc, d)
    r = run(nc, [{"in_" + n: x for n, x in arrays.items()}], core_ids=[0])
    return np.ascontiguousarray(np.asarray(r.results[0]["out"]).reshape(D, S).T)[None]
```
